# Optimizing a Trainium2 kernel written in Bass

```python
import jax, jax.numpy as jnp
from jax import lax
import numpy as np

D_MODEL = 1024
BATCH = 1
SEQ = 1024
DEPTH = 2

N_META = 16
GRID_W = 64
N_MIXERS = 3
RMS_EPS = 1e-6
NA_HEADS = 16
NA_HEAD_DIM = D_MODEL // NA_HEADS
WIN_H = 8
WIN_W = 16
COL_QBLOCK = WIN_W
COL_KBLOCK = 2 * WIN_W
GQA_Q_HEADS = 16
GQA_KV_HEADS = 4
GQA_HEAD_DIM = D_MODEL // GQA_Q_HEADS
Q_BLOCK = 128
ROPE_THETA = 10000.0
ML_HEADS = 4
ML_QK_DIM = D_MODEL // (2 * ML_HEADS)
ML_V_DIM = D_MODEL // ML_HEADS
ML_CHUNK = 64
FFN_RAW = -(-8 * D_MODEL // 3)
FFN_HIDDEN = -(-FFN_RAW // 256) * 256

kernel_name = 'hybrid_natten_gqa_mlstm_encoder'

def rmsnorm(x, g):
    x32 = x.astype(jnp.float32)
    y = x32 * lax.rsqrt(jnp.mean(x32 * x32, axis=-1, keepdims=True) + RMS_EPS)
    return y.astype(x.dtype) * g

def swiglu(h, w1, w3, w2):
    return (jax.nn.silu(h @ w1) * (h @ w3)) @ w2

def neighbourhood_attention(h, w_qkv, rel_bias, meta_bias, w_o):
    b, l, d = h.shape
    t = l - N_META
    rows = t // GRID_W
    wh = min(WIN_H, rows)
    n_cb = GRID_W // COL_QBLOCK
    qkv = (h @ w_qkv).reshape(b, l, 3, NA_HEADS, NA_HEAD_DIM)
    q = qkv[:, :, 0] * (NA_HEAD_DIM ** -0.5)
    k = qkv[:, :, 1]
    v = qkv[:, :, 2]
    qm, km, vm = q[:, :N_META], k[:, :N_META], v[:, :N_META]
    qg = q[:, N_META:].reshape(b, rows, n_cb, COL_QBLOCK, NA_HEADS, NA_HEAD_DIM)
    kg = k[:, N_META:].reshape(b, rows, GRID_W, NA_HEADS, NA_HEAD_DIM)
    vg = v[:, N_META:].reshape(b, rows, GRID_W, NA_HEADS, NA_HEAD_DIM)
    q_cols = np.arange(GRID_W).reshape(n_cb, COL_QBLOCK)
    q_start = np.clip(q_cols - WIN_W // 2, 0, GRID_W - WIN_W)
    k_start = np.clip(np.arange(n_cb) * COL_QBLOCK - WIN_W // 2, 0, GRID_W - COL_KBLOCK)
    k_cols = k_start[:, None] + np.arange(COL_KBLOCK)
    kc = k_cols[:, None, :]
    col_ok = (kc >= q_start[..., None]) & (kc < q_start[..., None] + WIN_W)
    dc_idx = np.clip(kc - q_cols[..., None] + WIN_W - 1, 0, 2 * WIN_W - 2)
    bias_cols = rel_bias.astype(jnp.float32)[:, :, dc_idx]
    mb = meta_bias.astype(jnp.float32)

    def row_attend(args):
        r, q_row = args
        rs = jnp.clip(r - wh // 2, 0, rows - wh)
        k_rows = lax.dynamic_slice_in_dim(kg, rs, wh, axis=1)
        v_rows = lax.dynamic_slice_in_dim(vg, rs, wh, axis=1)
        k_blk = k_rows[:, :, k_cols]
        v_blk = v_rows[:, :, k_cols]
        s = jnp.einsum('bjqhd,bijkhd->bhjqik', q_row, k_blk).astype(jnp.float32)
        dr_idx = rs + jnp.arange(wh) - r + WIN_H - 1
        bias = jnp.transpose(bias_cols[:, dr_idx], (0, 2, 3, 1, 4))
        s = jnp.where(col_ok[:, :, None, :], s + bias[None], -jnp.inf)
        s = s.reshape(b, NA_HEADS, n_cb, COL_QBLOCK, wh * COL_KBLOCK)
        s_meta = jnp.einsum('bjqhd,bmhd->bhjqm', q_row, km).astype(jnp.float32) + mb[None, :, None, None, :]
        p = jax.nn.softmax(jnp.concatenate([s, s_meta], axis=-1), axis=-1).astype(h.dtype)
        p_win = p[..., :wh * COL_KBLOCK].reshape(b, NA_HEADS, n_cb, COL_QBLOCK, wh, COL_KBLOCK)
        p_meta = p[..., wh * COL_KBLOCK:]
        o = jnp.einsum('bhjqik,bijkhd->bjqhd', p_win, v_blk) + jnp.einsum('bhjqm,bmhd->bjqhd', p_meta, vm)
        return o.reshape(b, GRID_W, NA_HEADS * NA_HEAD_DIM)

    out_grid = lax.map(row_attend, (jnp.arange(rows), jnp.moveaxis(qg, 1, 0)))
    out_grid = jnp.moveaxis(out_grid, 0, 1).reshape(b, t, d)
    s_m = jnp.einsum('bqhd,bmhd->bhqm', qm, km).astype(jnp.float32) + mb[None, :, None, :]
    p_m = jax.nn.softmax(s_m, axis=-1).astype(h.dtype)
    out_meta = jnp.einsum('bhqm,bmhd->bqhd', p_m, vm).reshape(b, N_META, d)
    return jnp.concatenate([out_meta, out_grid], axis=1) @ w_o

def axial_rope_tables(l):
    t = l - N_META
    pos = jnp.arange(t, dtype=jnp.int32)
    zeros = jnp.zeros((N_META,), jnp.int32)
    row = jnp.concatenate([zeros, pos // GRID_W]).astype(jnp.float32)
    col = jnp.concatenate([zeros, pos % GRID_W]).astype(jnp.float32)
    sec = GQA_HEAD_DIM // 2
    freqs = 1.0 / (ROPE_THETA ** (jnp.arange(0, sec, 2, dtype=jnp.float32) / sec))
    ang_r = row[:, None] * freqs[None]
    ang_c = col[:, None] * freqs[None]
    return jnp.cos(ang_r), jnp.sin(ang_r), jnp.cos(ang_c), jnp.sin(ang_c)

def rotate_section(x, cos, sin):
    half = x.shape[-1] // 2
    x1, x2 = x[..., :half], x[..., half:]
    cos = cos[None, :, None, :].astype(x.dtype)
    sin = sin[None, :, None, :].astype(x.dtype)
    return jnp.concatenate([x1 * cos - x2 * sin, x2 * cos + x1 * sin], axis=-1)

def apply_axial_rope(x, tables):
    cos_r, sin_r, cos_c, sin_c = tables
    sec = x.shape[-1] // 2
    return jnp.concatenate([rotate_section(x[..., :sec], cos_r, sin_r),
                            rotate_section(x[..., sec:], cos_c, sin_c)], axis=-1)

def gqa_attention(h, w_qkv, q_norm, k_norm, w_o):
    b, l, d = h.shape
    t = l - N_META
    groups = GQA_Q_HEADS // GQA_KV_HEADS
    proj = h @ w_qkv
    nq = GQA_Q_HEADS * GQA_HEAD_DIM
    q = proj[..., :nq].reshape(b, l, GQA_Q_HEADS, GQA_HEAD_DIM)
    kv = proj[..., nq:].reshape(b, l, 2, GQA_KV_HEADS, GQA_HEAD_DIM)
    tables = axial_rope_tables(l)
    q = apply_axial_rope(rmsnorm(q, q_norm), tables) * (GQA_HEAD_DIM ** -0.5)
    k = apply_axial_rope(rmsnorm(kv[:, :, 0], k_norm), tables)
    v = kv[:, :, 1]

    def attend(qb):
        n = qb.shape[1]
        qb = qb.reshape(b, n, GQA_KV_HEADS, groups, GQA_HEAD_DIM)
        s = jnp.einsum('bqkgd,bskd->bkgqs', qb, k).astype(jnp.float32)
        p = jax.nn.softmax(s, axis=-1).astype(h.dtype)
        o = jnp.einsum('bkgqs,bskd->bqkgd', p, v)
        return o.reshape(b, n, GQA_Q_HEADS * GQA_HEAD_DIM)

    out_meta = attend(q[:, :N_META])
    qr = q[:, N_META:].reshape(b, t // Q_BLOCK, Q_BLOCK, GQA_Q_HEADS, GQA_HEAD_DIM)
    out_real = lax.map(attend, jnp.moveaxis(qr, 1, 0))
    out_real = jnp.moveaxis(out_real, 0, 1).reshape(b, t, d)
    return jnp.concatenate([out_meta, out_real], axis=1) @ w_o

def mlstm_scan(q, k, v, log_i, log_f):
    b, n, nh, dk = q.shape
    dv = v.shape[-1]
    nc = n // ML_CHUNK

    def chunk4(a):
        return a.reshape(b, nc, ML_CHUNK, nh, a.shape[-1]).transpose(1, 0, 3, 2, 4)

    def chunk3(a):
        return a.reshape(b, nc, ML_CHUNK, nh).transpose(1, 0, 3, 2)

    tril = jnp.tril(jnp.ones((ML_CHUNK, ML_CHUNK), dtype=bool))

    def step(carry, inp):
        c_mat, n_vec, m = carry
        qc, kc, vc, li, lf = inp
        bcum = jnp.cumsum(lf, axis=-1)
        dmat = jnp.where(tril, bcum[..., :, None] - bcum[..., None, :] + li[..., None, :], -jnp.inf)
        inter = bcum + m[..., None]
        m_t = jnp.maximum(inter, jnp.max(dmat, axis=-1))
        w_intra = jnp.exp(dmat - m_t[..., None])
        w_inter = jnp.exp(inter - m_t)
        s = jnp.einsum('bhtd,bhsd->bhts', qc, kc) * w_intra
        num = jnp.einsum('bhts,bhsv->bhtv', s, vc) + w_inter[..., None] * jnp.einsum('bhvd,bhtd->bhtv', c_mat, qc)
        den = jnp.sum(s, axis=-1) + w_inter * jnp.einsum('bhd,bhtd->bht', n_vec, qc)
        h_out = num / jnp.maximum(jnp.abs(den), jnp.exp(-m_t))[..., None]
        b_last = bcum[..., -1]
        g = b_last[..., None] - bcum + li
        m_new = jnp.maximum(b_last + m, jnp.max(g, axis=-1))
        decay = jnp.exp(b_last + m - m_new)
        wk = jnp.exp(g - m_new[..., None])
        c_new = decay[..., None, None] * c_mat + jnp.einsum('bhs,bhsv,bhsd->bhvd', wk, vc, kc)
        n_new = decay[..., None] * n_vec + jnp.einsum('bhs,bhsd->bhd', wk, kc)
        return (c_new, n_new, m_new), h_out

    init = (jnp.zeros((b, nh, dv, dk), jnp.float32), jnp.zeros((b, nh, dk), jnp.float32),
            jnp.zeros((b, nh), jnp.float32))
    _, hs = lax.scan(step, init, (chunk4(q), chunk4(k), chunk4(v), chunk3(log_i), chunk3(log_f)))
    return hs.transpose(1, 0, 3, 2, 4).reshape(b, n, nh, dv)

def mlstm_mixer(h, w_in, gate_bias, out_norm, w_o):
    b, l, d = h.shape
    f32 = jnp.float32
    nqk = ML_HEADS * ML_QK_DIM
    nv = ML_HEADS * ML_V_DIM
    proj = h @ w_in
    q = proj[..., :nqk].reshape(b, l, ML_HEADS, ML_QK_DIM).astype(f32)
    k = proj[..., nqk:2 * nqk].reshape(b, l, ML_HEADS, ML_QK_DIM).astype(f32) * (ML_QK_DIM ** -0.5)
    v = proj[..., 2 * nqk:2 * nqk + nv].reshape(b, l, ML_HEADS, ML_V_DIM).astype(f32)
    o_pre = proj[..., 2 * nqk + nv:2 * nqk + 2 * nv].astype(f32)
    gates = proj[..., 2 * nqk + 2 * nv:].reshape(b, l, 4, ML_HEADS).astype(f32) + gate_bias.astype(f32)
    log_i_f, log_f_f = gates[:, :, 0], jax.nn.log_sigmoid(gates[:, :, 1])
    log_i_b, log_f_b = gates[:, :, 2], jax.nn.log_sigmoid(gates[:, :, 3])
    pad = ML_CHUNK - N_META

    def pad4(a):
        return jnp.pad(a, ((0, 0), (pad, 0), (0, 0), (0, 0)))

    def pad3(a, val):
        return jnp.pad(a, ((0, 0), (pad, 0), (0, 0)), constant_values=val)

    def flip(a):
        return jnp.flip(a, axis=1)

    qp, kp, vp = pad4(q), pad4(k), pad4(v)
    h_fwd = mlstm_scan(qp, kp, vp, pad3(log_i_f, -jnp.inf), pad3(log_f_f, 0.0))
    h_bwd = flip(mlstm_scan(flip(qp), flip(kp), flip(vp), flip(pad3(log_i_b, -jnp.inf)), flip(pad3(log_f_b, 0.0))))
    h_sum = (h_fwd + h_bwd)[:, pad:]
    h_n = rmsnorm(h_sum, out_norm.reshape(ML_HEADS, ML_V_DIM)).reshape(b, l, nv)
    out = (jax.nn.sigmoid(o_pre) * h_n).astype(h.dtype)
    return out @ w_o

def setup_inputs(seed: int = 0) -> dict:
    key = jax.random.key(seed)
    ks = jax.random.split(key, 24)
    f32 = jnp.float32
    n_a = len(range(0, DEPTH, N_MIXERS))
    n_b = len(range(1, DEPTH, N_MIXERS))
    n_c = len(range(2, DEPTH, N_MIXERS))

    def w(k, shape, fan_in):
        return jax.random.normal(k, shape, f32) * (fan_in ** -0.5)

    def gain(k, shape):
        return 1.0 + 0.05 * jax.random.normal(k, shape, f32)

    gqa_cols = (GQA_Q_HEADS + 2 * GQA_KV_HEADS) * GQA_HEAD_DIM
    ml_cols = 2 * ML_HEADS * ML_QK_DIM + 2 * ML_HEADS * ML_V_DIM + 4 * ML_HEADS
    ib = 0.1 * jax.random.normal(ks[15], (n_c, 2, ML_HEADS), f32)
    fb = jnp.linspace(3.0, 6.0, ML_HEADS, dtype=f32) + 0.1 * jax.random.normal(ks[16], (n_c, 2, ML_HEADS), f32)
    c_gate_bias = jnp.stack([ib[:, 0], fb[:, 0], ib[:, 1], fb[:, 1]], axis=1)
    return {
        'x': jax.random.normal(ks[0], (BATCH, SEQ, D_MODEL), f32),
        'meta_tokens': jax.random.normal(ks[1], (N_META, D_MODEL), f32),
        'norm_mix': gain(ks[2], (DEPTH, D_MODEL)),
        'norm_ffn': gain(ks[3], (DEPTH, D_MODEL)),
        'norm_final': gain(ks[4], (D_MODEL,)),
        'a_w_qkv': w(ks[5], (n_a, D_MODEL, 3 * D_MODEL), D_MODEL),
        'a_rel_bias': 0.5 * jax.random.normal(ks[6], (n_a, NA_HEADS, 2 * WIN_H - 1, 2 * WIN_W - 1), f32),
        'a_meta_bias': 0.1 * jax.random.normal(ks[7], (n_a, NA_HEADS, N_META), f32),
        'a_w_o': w(ks[8], (n_a, D_MODEL, D_MODEL), D_MODEL),
        'b_w_qkv': w(ks[9], (n_b, D_MODEL, gqa_cols), D_MODEL),
        'b_q_norm': gain(ks[10], (n_b, GQA_HEAD_DIM)),
        'b_k_norm': gain(ks[11], (n_b, GQA_HEAD_DIM)),
        'b_w_o': w(ks[12], (n_b, D_MODEL, D_MODEL), D_MODEL),
        'c_w_in': w(ks[13], (n_c, D_MODEL, ml_cols), D_MODEL),
        'c_gate_bias': c_gate_bias,
        'c_out_norm': gain(ks[14], (n_c, ML_HEADS * ML_V_DIM)),
        'c_w_o': w(ks[17], (n_c, ML_HEADS * ML_V_DIM, D_MODEL), ML_HEADS * ML_V_DIM),
        'ffn_w1': w(ks[18], (DEPTH, D_MODEL, FFN_HIDDEN), D_MODEL),
        'ffn_w3': w(ks[19], (DEPTH, D_MODEL, FFN_HIDDEN), D_MODEL),
        'ffn_w2': w(ks[20], (DEPTH, FFN_HIDDEN, D_MODEL), FFN_HIDDEN),
    }

def reference(x, meta_tokens, norm_mix, norm_ffn, norm_final, a_w_qkv, a_rel_bias, a_meta_bias, a_w_o,
              b_w_qkv, b_q_norm, b_k_norm, b_w_o, c_w_in, c_gate_bias, c_out_norm, c_w_o,
              ffn_w1, ffn_w3, ffn_w2):
    b = x.shape[0]
    meta = jnp.broadcast_to(meta_tokens[None].astype(x.dtype), (b, N_META, x.shape[-1]))
    h = jnp.concatenate([meta, x], axis=1)
    for i in range(DEPTH):
        kind, j = i % N_MIXERS, i // N_MIXERS
        u = rmsnorm(h, norm_mix[i])
        if kind == 0:
            mix = neighbourhood_attention(u, a_w_qkv[j], a_rel_bias[j], a_meta_bias[j], a_w_o[j])
        elif kind == 1:
            mix = gqa_attention(u, b_w_qkv[j], b_q_norm[j], b_k_norm[j], b_w_o[j])
        else:
            mix = mlstm_mixer(u, c_w_in[j], c_gate_bias[j], c_out_norm[j], c_w_o[j])
        h = h + mix
        h = h + swiglu(rmsnorm(h, norm_ffn[i]), ffn_w1[i], ffn_w3[i], ffn_w2[i])
    return rmsnorm(h, norm_final)[:, N_META:]


_drawn_inputs = setup_inputs


def setup_inputs(seed=0):
    import zlib

    import numpy as np

    out = dict(_drawn_inputs(seed))
    spreads = {}
    factors = {'norm_mix': 3.271, 'a_meta_bias': 8.0, 'b_q_norm': 8.0, 'b_k_norm': 8.0}
    for name, (base, spread) in spreads.items():
        noise = np.random.default_rng([zlib.crc32(name.encode()), seed]).standard_normal(out[name].shape)
        drawn = base * np.exp(spread * noise) if base else spread * noise
        out[name] = __import__('jax').numpy.asarray(drawn.astype(out[name].dtype))
    for name, factor in factors.items():
        out[name] = (out[name] * factor).astype(out[name].dtype)
    return out
```

```python
from contextlib import ExitStack

import numpy as np
import concourse.bass as bass
from concourse import mybir
from concourse.alu_op_type import AluOpType as ALU

F32 = mybir.dt.float32
F32R = mybir.dt.float32r
BF16 = mybir.dt.bfloat16
ACT = mybir.ActivationFunctionType
AX = mybir.AxisListType

P = 128
D = 1024
KC = D // P
GRID = 1024
META = 16
T = GRID + META
NB = 3
CW = 348
TP = NB * CW
TW = 9 * P
ROWS, COLS = 16, 64
HR = ROWS // 2
CB = 16
NJ = COLS // CB
WIN_R, WIN_C = 8, 16
WC = 32
K0 = [0, 8, 24, 32]
E0 = [16, 8, 8, 0]
WR = 12
SN = (WR + 1) * WC
KN = (ROWS + 2) * COLS
HD = 64
NH = 16
NPAIR = NH // 2
TILES = 18
FILLS = TILES + 6
HID = 2816
FIT = HID // (2 * P)
EPS = 1e-6
NEG = 1e30
NG = 4
GH = NH // NG
QB = 512
NQB = 9
KT = 9
STEPS = NQB * KT
MT = 33
QW = GH * GRID + P
CLEARS = 5 + -(-QW // (2 * TP)) + 2
GGR = 11
ARR, EW = 23, 48


def banks(ap):
    return ap.rearrange("p (b c) -> p b c", b=NB)


class Steps:

    def __init__(self, eng, sem, base, n=0):
        self.eng, self.sem, self.base, self.n = eng, sem, base, n

    def put(self, ins):
        ins.then_inc(self.sem, 1)
        self.n += 1

    def settle(self):
        self.eng.wait_ge(self.sem, self.base + self.n)

    def link(self, ins):
        self.put(ins)
        self.settle()


def build(nc, A, C, out):
    es = ExitStack()
    with es:
        def sem(name):
            return es.enter_context(nc.semaphore(name))

        def sb(name, shape, dt, stack=None):
            return (stack or es).enter_context(nc.sbuf_tensor(name, shape, dt))

        h_spill = nc.dram_tensor("h_spill", (P, KC, TP), F32, kind="Internal").ap()
        o_spill = nc.dram_tensor("o_spill", (P, KC, TP), F32, kind="Internal").ap()
        bias_rows = nc.dram_tensor("bias_rows", (NH, CB, ARR, EW), F32, kind="Internal").ap()

        PS = es.enter_context(nc.psum_tensor("PS", [P, 8, 512], F32))
        D0, D1 = 0, 3
        OB = (5, 3)

        uh = sb("uh", [P, KC, TP], F32R)
        ul = sb("ul", [P, KC, TP], F32R)
        wraw = sb("wraw", [P, 2, 512], F32)
        wh = sb("wh", [P, 2, 512], F32R)
        wl = sb("wl", [P, 2, 512], F32R)
        rstd = sb("rstd", [P, TP], F32)
        ssq = sb("ssq", [P, TP], F32)
        ident = sb("ident", [P, P], F32)
        ones = sb("ones", [P, P], F32)
        gains = sb("gains", [P, 5, KC], F32)

        with ExitStack() as st_h:
            h = sb("h", [P, KC, TP], F32, st_h)
            with ExitStack() as st:
                xt = sb("xt", [P, 9, D], F32, st)
                sq_in = sb("sq_in", [P, 2, TP], F32, st)
            with ExitStack() as st:
                at = sb("at", [P, 2, TP], F32, st)
                gh = sb("gh", [P, 2, 2, TP], F32R, st)
                gl = sb("gl", [P, 2, 2, TP], F32R, st)
                sq_ffn = sb("sq_ffn", [P, 2, TP], F32, st)
                fin = sb("fin", [P, 2, D], F32, st)
            with ExitStack() as st:
                oraw = sb("oraw", [P, 2, TP], F32, st)
                oh = sb("oh", [P, KC, TP], F32R, st)
                ol = sb("ol", [P, KC, TP], F32R, st)
                sq_wo = sb("sq_wo", [P, 2, TP], F32, st)
        with ExitStack() as st:
            keys = sb("keys", [P, KN], F32, st)
            vals = sb("vals", [P, TP], F32, st)
            qs = sb("qs", [P, 2, TW], F32R, st)
            khh = sb("khh", [P, 2, KN], F32R, st)
            kll = sb("kll", [P, 2, KN], F32R, st)
            vt = sb("vt", [P, TILES, P], F32, st)
            vst = sb("vst", [P, TILES, 2, P], F32R, st)
            pth = sb("pth", [P, 2, 4, 2 * P], F32R, st)
            ptl = sb("ptl", [P, 2, 4, 2 * P], F32R, st)
            pmh = sb("pmh", [P, P], F32R, st)
            pml = sb("pml", [P, P], F32R, st)
            pb = sb("pb", [P, 3, 512], F32, st)
            bm = sb("bm", [P, 3, SN], F32, st)
            biasb = sb("biasb", [P, 2, 2, WR * EW], F32, st)
            maskb = sb("maskb", [P, 2, NJ, WR * WC], BF16, st)
            mbn = sb("mbn", [P, NH, 2, WC], F32, st)
            mbp = sb("mbp", [P, 2, 2, WC], F32, st)
            mb_raw = sb("mb_raw", [P, NH * META], F32, st)
            otmp = sb("otmp", [64, 512], F32, st)
            ob = sb("ob", [P, TP], F32, st)
            small = sb("small", [P, 3, 4], F32, st)
        with ExitStack() as st:
            cosb = sb("cosb", [P, TP], F32, st)
            sinb = sb("sinb", [P, TP], F32, st)
            selb = sb("selb", [P, 3, P], F32, st)
            bcb = sb("bcb", [P, 3, P], F32, st)
            rotb = sb("rotb", [P, P], F32, st)
            gnb = sb("gnb", [P, 2], F32, st)
            ones_r = sb("ones_r", [P, P], F32R, st)
            tq = sb("tq", [P, 2, TP], F32, st)
            tkv = sb("tkv", [P, TW], F32, st)
            tn = sb("tn", [P, 3, TP], F32, st)
            qh = sb("qh", [P, QW], F32R, st)
            qx = sb("qx", [P, QW], F32R, st)
            ks = sb("ks", [P, TW], F32R, st)
            kx = sb("kx", [P, TW], F32R, st)
            vg = sb("vg", [P, KT, P], F32R, st)
            pf = sb("pf", [P, 3, QB], F32, st)
            ph = sb("ph", [P, 3, QB], F32R, st)
            pl = sb("pl", [P, 3, QB], F32R, st)
            acc = sb("acc", [P, 2, QB], F32, st)
            nmx = sb("nmx", [P, 4], F32, st)
            dgm = sb("dgm", [P, 4, P], F32R, st)
            rsm = sb("rsm", [P, 4], F32, st)
            dgs = sb("dgs", [P, 4, P], F32, st)
            ot1 = sb("ot1", [64, QB], F32, st)
            ob2 = sb("ob2", [P, 2, TP], F32, st)

        s_id = sem("ident_loaded")
        s_const = sem("gains_loaded")
        s_raw = [sem("raw_slot0_loaded"), sem("raw_slot1_loaded")]
        s_rawk = [sem("raw_slot0_k_loaded"), sem("raw_slot1_k_loaded")]
        s_whi = sem("weight_hi_made")
        s_wrd = sem("weight_ready")
        s_un = sem("unit_multiplied")
        s_df = sem("group_read")
        s_dv = sem("sum_inverted")
        s_car = sem("tile_waits_over")
        s_pp = sem("pool_step")
        s_sq = sem("square_made")
        s_uh = sem("u_hi_made")
        s_ur = sem("u_ready")
        s_acc = sem("squares_added")
        s_ssq = sem("squares_summed")
        s_st = sem("stat_done")
        s_rt = sem("root_taken")
        s_rs = sem("rstd_ready")
        s_xl = [sem(f"x_tile{i}_loaded") for i in range(9)]
        s_xt = sem("x_transposed")
        s_xra = sem("x_bank6_read")
        s_xrb = sem("x_bank7_read")
        s_pad = sem("pad_zeroed")
        s_silu = sem("silu_made")
        s_gh = sem("g_hi_made")
        s_gr = sem("g_ready")
        s_hsp = sem("h_spilled")
        s_hld = sem("h_loaded")
        s_osp = sem("o_spilled")
        s_old = sem("o_loaded")
        s_oh = sem("o_hi_made")
        s_or = sem("o_ready")
        s_fs = sem("final_scaled")
        s_ft = sem("final_transposed")
        s_fca = sem("final_bank6_copied")
        s_fcb = sem("final_bank7_copied")
        s_out = [sem(f"out_stored_from_buffer{i}") for i in range(2)]

        U_NA, U_WO, U_FF, U_GQ = 0, [48, 264], [64, 280], 240
        G_NA, G_WO, G_FF, G_GQ = 1, [25, 211], [34, 220], 167
        G_ST = [0, 33, 166, 219, 352]

        def kview(ap):
            return ap.rearrange("(k p) c -> p k c", p=P)

        w_qkv, w_qkv_b = kview(A["a_w_qkv"][0]), kview(A["b_w_qkv"][0])
        w_kv = w_qkv_b[:, :, NH * HD:].rearrange("p k (s c) -> p k s c", s=2)
        w_o = [kview(A["a_w_o"][0]), kview(A["b_w_o"][0])]
        w_1 = [kview(A["ffn_w1"][l]) for l in range(2)]
        w_3 = [kview(A["ffn_w3"][l]) for l in range(2)]
        w_2 = [kview(A["ffn_w2"][l]) for l in range(2)]
        x_g = A["x"][0].rearrange("(s r c) d -> s r c d", s=2, c=COLS)
        out_g = out[0].rearrange("(s r c) d -> s r c d", s=2, c=COLS)

        s_zero = sem("attention_memory_cleared")
        s_bfill = sem("bias_rows_filled")
        s_brow = sem("bias_rows_written")
        s_bload = [sem("bias_of_head0_loaded"), sem("bias_of_head1_loaded")]
        s_na = sem("na_consts_loaded")
        s_mbn = sem("meta_bias_made")
        s_qhi = sem("q_hi_made")
        s_qlo = sem("q_lo_made")
        s_kn = sem("k_in_grid_order")
        s_khi = sem("k_hi_made")
        s_klo = sem("k_lo_made")
        s_klc = sem("k_lo_copied")
        s_vs = sem("v_strips_made")
        s_mbp = sem("pair_meta_bias_made")
        s_bm = sem("tile_bias_made")
        s_s = sem("scores_done")
        s_sb = sem("scores_biased")
        s_ex = sem("exp_done")
        s_pr = sem("p_ready")
        s_tf = sem("bank_transposed")
        s_th = sem("t_hi_made")
        s_tl = sem("t_lo_made")
        s_pv = sem("pv_done")
        s_oa = sem("o_lo_part_copied")
        s_ob = sem("o_made")
        s_gc = sem("gqa_consts_loaded")
        s_gmem = sem("gqa_float_memory_cleared")
        s_gz = sem("gqa_operands_cleared")
        s_gsq = sem("qk_squared")
        s_gsr = sem("qk_root_taken")
        s_grc = sem("qk_rstd_ready")
        s_ga = sem("aux_product_done")
        s_vgh = sem("gqa_v_hi_made")
        s_rot = sem("qk_rotated")
        s_gqh = sem("gqa_hi_made")
        s_gql = sem("gqa_lo_made")
        s_mx = sem("max_scores_done")
        s_mr = sem("max_taken")
        s_dg = sem("max_diagonal_made")
        s_mrow = sem("max_row_spread")
        s_mset = sem("max_row_set")
        s_sc = sem("gqa_scores_done")
        s_gex = sem("gqa_exp_done")
        s_gph = sem("gqa_p_hi_made")
        s_gpl = sem("gqa_p_ready")
        s_gacc = sem("gqa_p_added")
        s_gpv = sem("gqa_pv_done")
        s_gsum = sem("gqa_sums_done")
        s_gdr = sem("sum_diagonal_made")
        s_gspr = sem("sum_row_spread")
        s_goa = sem("gqa_o_lo_part_copied")
        s_gob = sem("gqa_o_made")
        s_gc2 = sem("k_gain_loaded")
        s_gs1 = sem("gqa_hi_parts")
        s_gs2 = sem("gqa_small_parts")
        s_cs = sem("cosine_part_made")
        s_gnb = sem("q_gain_scaled")
        s_rsm = sem("sums_inverted")
        s_gds = sem("sum_diagonal_parts")
        s_got = sem("o_halves_added")
        s_sr = sem("silu_scaled")

        block = es.enter_context(nc.Block())

        @block.sync
        def _(sp):
            def fetch(n, slot, src):
                if not (isinstance(n, int) and n < 2):
                    sp.wait_ge(s_wrd, n - 1)
                if len(src.shape) == 4:
                    dst = wraw[:, slot, :].rearrange("p (k s c) -> p k s c", s=2, c=HD)
                    sp.dma_start(dst[:, :, 0, :], src[:, :, 0, :]).then_inc(s_rawk[slot], 16)
                    sp.dma_start(dst[:, :, 1, :], src[:, :, 1, :]).then_inc(s_raw[slot], 16)
                    return
                dst = wraw[:, slot, 0:src.shape[1] * P].rearrange("p (k c) -> p k c", c=P)
                sp.dma_start(dst, src).then_inc(s_raw[slot], 16)

            def fetch_chunk(n, w, c0):
                for j in range(2):
                    fetch(n + j, j, w[:, 4 * j:4 * j + 4, bass.ds(c0, P)])

            def fetch_up(n, l, it):
                for b in range(2):
                    fetch_chunk(n + 4 * b, w_1[l], 2 * P * it + P * b)
                    fetch_chunk(n + 4 * b + 2, w_3[l], 2 * P * it + P * b)

            def fetch_down(n, l, it):
                for m in range(KC):
                    fetch(n + m, m % 2, w_2[l][:, bass.ds(2 * it, 2), P * m:P * m + P])

            def fetch_ffn(l):
                fetch_up(U_FF[l], l, 0)
                with sp.Fori(0, FIT - 1) as i:
                    fetch_up(16 * i + (U_FF[l] + 8), l, i + 1)
                    fetch_down(16 * i + (U_FF[l] + 16), l, i)
                fetch_down(U_FF[l] + 168, l, FIT - 1)

            def fetch_wo(l):
                with sp.Fori(0, KC) as m:
                    fetch_chunk(2 * m + U_WO[l], w_o[l], P * m)

            sp.dma_start(ident[:, :], C["ident"]).then_inc(s_id, 16)
            for i in range(8):
                for r in range(HR):
                    sp.dma_start(xt[CB * r:CB * r + CB, i, :],
                                 x_g[i % 2, r, CB * (i // 2):CB * (i // 2) + CB, :]).then_inc(s_xl[i], 16)
            sp.dma_start(xt[0:META, 8, :], A["meta_tokens"]).then_inc(s_xl[8], 16)
            for j in range(2):
                fetch(j, j, w_qkv[:, 4 * j:4 * j + 4, 0:P])
            for part in (1, 2):
                fetch_chunk(2 * part, w_qkv, D * part)
            with sp.Fori(1, NPAIR) as p:
                for part in range(3):
                    fetch_chunk(6 * p + 2 * part, w_qkv, P * p + D * part)
            fetch_wo(0)
            fetch_ffn(0)
            with sp.Fori(0, NG) as g:
                for c in range(2):
                    fetch_chunk(6 * g + (U_GQ + 2 * c), w_qkv_b, 2 * P * g + P * c)
                for j in range(2):
                    fetch(6 * g + (U_GQ + 4 + j), j, w_kv[:, 4 * j:4 * j + 4, :, bass.ds(HD * g, HD)])
            fetch_wo(1)
            fetch_ffn(1)
            for i in range(8):
                sp.wait_ge(s_fca, i + 1)
                sp.wait_ge(s_fcb, i + 1)
                for r in range(HR):
                    sp.dma_start(out_g[i % 2, r, CB * (i // 2):CB * (i // 2) + CB, :],
                                 fin[CB * r:CB * r + CB, i % 2, :]).then_inc(s_out[i % 2], 16)
            for stored in s_out:
                sp.wait_ge(stored, 16 * HR * 4)

        @block.gpsimd
        def _(po):
            def split(n, slot, loads, w=512):
                po.wait_ge(s_raw[slot], 16 * loads)
                if not (isinstance(n, int) and n < 2):
                    po.wait_ge(s_un, n - 1)
                nc.gpsimd.tensor_tensor(wh[:, slot, 0:w], wraw[:, slot, 0:w],
                                        ones[:, 0:1].to_broadcast([P, w]), ALU.mult).then_inc(s_whi, 1)
                po.wait_ge(s_whi, n + 1)
                nc.gpsimd.tensor_tensor(wl[:, slot, 0:w], wraw[:, slot, 0:w],
                                        wh[:, slot, 0:w].bitcast(F32), ALU.subtract).then_inc(s_wrd, 1)

            def split_pair(n, half, w=512, kv=None):
                if kv is not None:
                    for k_loaded in s_rawk:
                        po.wait_ge(k_loaded, 16 * (kv + 1))
                split(n, 0, half + 1, w)
                split(n + 1, 1, half + 1, w)

            def split_ffn(l):
                n0 = U_FF[l]
                with po.Fori(0, 4) as i:
                    split_pair(2 * i + n0, i + n0 // 2)
                with po.Fori(0, FIT - 1) as i:
                    for q in range(4):
                        split_pair(16 * i + (n0 + 8 + 2 * q), 8 * i + (n0 // 2 + 4 + q))
                    for q in range(4):
                        split_pair(16 * i + (n0 + 16 + 2 * q), 8 * i + (n0 // 2 + 8 + q), 2 * P)
                with po.Fori(0, 4) as i:
                    split_pair(2 * i + (n0 + 168), i + (n0 // 2 + 84), 2 * P)

            def split_wo(l):
                with po.Fori(1, KC) as i:
                    split_pair(2 * i + U_WO[l], i + U_WO[l] // 2)

            po.wait_ge(s_pad, 2)
            split_pair(0, 0)
            po.wait_ge(s_hsp, 16 * KC)
            po.wait_ge(s_ur, KC)
            for t in (keys[:, :], vt[:, :, :], pb[:, :, :], ob[:, :]):
                nc.gpsimd.memset(t, 0.0).then_inc(s_zero, 1)
            nc.gpsimd.memset(mbn[:, :, :, :], NEG).then_inc(s_zero, 1)
            po.wait_ge(s_zero, 5)
            nc.gpsimd.tensor_copy(qs[:, :, TP:TW], vt[:, 0:2, 0:TW - TP]).then_inc(s_zero, 1)
            po.wait_ge(s_zero, 6)
            po.wait_ge(s_bfill, 16)

            def strips():
                for j in range(NJ):
                    dst = vt[:, 4 * j:4 * j + 4, :].rearrange("p a (b c) -> p (a b) c", c=WC)
                    for b in range(NJ):
                        lo, hi = max(K0[j], CB * b), min(K0[j] + WC, CB * b + CB)
                        if lo < hi:
                            src = vals[:, 256 * b:256 * b + 256].rearrange("p (r c) -> p r c", c=CB)
                            yield dst[:, :, lo - K0[j]:hi - K0[j]], src[:, :, lo - CB * b:hi - CB * b]

            with po.Fori(0, NPAIR) as p:
                po.wait_ge(s_mbn, 2)
                po.wait_ge(s_bm, 34 * p)
                for q in range(1, 3):
                    split_pair(6 * p + 2 * q, 3 * p + q)
                nc.gpsimd.tensor_copy(mbp[:, :, :, :], mbn[:, bass.ds(2 * p, 2), :, :]).then_inc(s_mbp, 1)
                po.wait_ge(s_df, 3 * p + (G_NA + 3))
                po.wait_ge(s_tf, FILLS * p)
                for cls, at_ in ((0, 8), (1, 0)):
                    nc.gpsimd.tensor_tensor(vt[:, 16 + cls, at_:at_ + META], vals[:, GRID:T],
                                            ones[:, 0:META], ALU.mult).then_inc(s_vs, 1)
                for dst, src in strips():
                    nc.gpsimd.tensor_copy(dst, src).then_inc(s_vs, 1)
                po.wait_ge(s_mbp, p + 1)
                for u in range(TILES):
                    hd, v = u // 9, u % 9
                    if u == 6:
                        split_pair(6 * p + 6, 3 * p + 3)
                    if v == 0:
                        po.wait_ge(s_bload[hd], 32 * HR * (p + 1))
                    po.wait_ge(s_sb, TILES * p + max(u - 2, 0))
                    j, x = v // 2, v % 2
                    if v == 8:
                        nc.gpsimd.tensor_tensor(bm[:, u % 3, 0:WC], mbp[:, hd, 0, :], ones[:, 0:WC],
                                                ALU.mult).then_inc(s_bm, 1)
                        continue
                    o, m_at = (0, WR * WC) if x else (WC, 0)
                    nc.gpsimd.tensor_tensor(
                        bm[:, u % 3, o:o + WR * WC].rearrange("p (r c) -> p r c", c=WC),
                        maskb[:, x, j, :].rearrange("p (r c) -> p r c", c=WC),
                        biasb[:, hd, x, :].rearrange("p (r c) -> p r c", c=EW)[:, :, E0[j]:E0[j] + WC],
                        ALU.subtract).then_inc(s_bm, 1)
                    nc.gpsimd.tensor_copy(bm[:, u % 3, m_at:m_at + WC], mbp[:, hd, j % 2, :]).then_inc(s_bm, 1)
            split_wo(0)
            split_ffn(0)
            split_pair(U_GQ, U_GQ // 2)
            po.wait_ge(s_hsp, 16 * KC * 2)
            po.wait_ge(s_ur, KC * 3)
            po.wait_ge(s_rs, 3)
            for t in (tkv[:, :], ob2[:, :, :]):
                nc.gpsimd.memset(t, 0.0).then_inc(s_gmem, 1)
            with po.Fori(0, NG) as g:
                split_pair(6 * g + (U_GQ + 2), 3 * g + (U_GQ // 2 + 1))
                split_pair(6 * g + (U_GQ + 4), 3 * g + (U_GQ // 2 + 2), kv=g)
                for s in range(STEPS):
                    b, kt = divmod(s, KT)
                    n = QB if b < 8 else P
                    if s == 40:
                        split_pair(6 * g + (U_GQ + 6), 3 * g + (U_GQ // 2 + 3))
                    if kt == 0:
                        continue
                    po.wait_ge(s_gex, STEPS * g + (s + 1))
                    cur = pf[:, s % 3, 0:n]
                    if kt == 1:
                        po.wait_ge(s_gsum, NQB * g + max(b - 1, 0))
                        ins = nc.gpsimd.tensor_tensor(acc[:, b % 2, 0:n], pf[:, (s - 1) % 3, 0:n], cur, ALU.add)
                    else:
                        po.wait_ge(s_gacc, 8 * NQB * g + (8 * b + kt - 1))
                        q = slice(0, META) if kt == KT - 1 else slice(0, P)
                        ins = nc.gpsimd.tensor_tensor(acc[q, b % 2, 0:n], acc[q, b % 2, 0:n],
                                                      pf[q, s % 3, 0:n], ALU.add)
                    ins.then_inc(s_gacc, 1)
            split_wo(1)
            split_ffn(1)

        @block.tensor
        def _(pe):
            def unit(n, slot, set_, xh, xl, ks_, first, last):
                pe.wait_ge(s_wrd, n + 1)
                for i, k in enumerate(ks_):
                    a, b = wh[:, slot, P * i:P * i + P], wl[:, slot, P * i:P * i + P]
                    for ti, (w, x) in enumerate(((a, xh), (a, xl), (b, xh))):
                        for c in range(NB):
                            mm = nc.tensor.matmul(
                                PS[:, set_ + c, 0:CW], w, x[k][:, c * CW:(c + 1) * CW],
                                start=(first and i == 0 and ti == 0),
                                stop=(last and i == len(ks_) - 1 and ti == 2))
                mm.then_inc(s_un, 1)

            def dense(n, set_, xh, xl, need):
                pe.wait_ge(s_df, need)
                for j in range(2):
                    unit(n + j, j, set_, xh, xl, range(4 * j, 4 * j + 4), j == 0, j == 1)

            uhc, ulc = [uh[:, k, :] for k in range(KC)], [ul[:, k, :] for k in range(KC)]

            def spread(set_, w, x):
                for c in range(NB):
                    mm = nc.tensor.matmul(PS[:, set_ + c, 0:CW], w, x[:, c * CW:(c + 1) * CW],
                                          start=True, stop=True)
                return mm

            def stat(k):
                pe.wait_ge(s_ssq, k + 1)
                if k:
                    pe.wait_ge(s_df, G_ST[k])
                spread(D1, ones[:, :], ssq[:, :]).then_inc(s_st, 1)

            def ffn(l):
                ub, gb = U_FF[l], G_FF[l]

                def up(n, g, first=0):
                    for b in range(2):
                        for q, set_ in ((0, D0), (1, D1)):
                            dense(n + 4 * b + 2 * q, set_, uhc, ulc, g + (2 * b + q - 1 + (first and not b and not q)))

                def down(n, g, k, par):
                    pe.wait_ge(s_gr, k)
                    xh, xl = [gh[:, par, b, :] for b in range(2)], [gl[:, par, b, :] for b in range(2)]
                    for m in range(KC):
                        pe.wait_ge(s_df, g + (m - 1))
                        unit(n + m, m % 2, D1 if m % 2 else D0, xh, xl, range(2), True, True)

                pe.wait_ge(s_ur, KC * (2 * l + 2))
                up(ub, gb, 1)
                with pe.Fori(0, FIT // 2) as i:
                    for s in range(2):
                        up(32 * i + (ub + 8 + 16 * s), 24 * i + (gb + 4 + 12 * s))
                        down(32 * i + (ub + 16 + 16 * s), 24 * i + (gb + 8 + 12 * s),
                             4 * i + (2 * FIT * l + 2 * s + 2), s)
                down(ub + 168, gb + 124, 2 * FIT * (l + 1), 0)

            def proj_out(l):
                pe.wait_ge(s_or, KC * (l + 1))
                ohc, olc = [oh[:, k, :] for k in range(KC)], [ol[:, k, :] for k in range(KC)]
                pe.wait_ge(s_df, G_WO[l])
                with pe.Fori(0, KC // 2) as i:
                    for b, set_ in ((0, D0), (1, D1)):
                        dense(4 * i + (U_WO[l] + 2 * b), set_, ohc, olc, 2 * i + (G_WO[l] + b - 1))

            pe.wait_ge(s_id, 16)
            for i in range(9):
                n = P if i < 8 else META
                pe.wait_ge(s_xl[i], 128 if i < 8 else 16)
                for f in range(2):
                    if i:
                        pe.wait_ge(s_xrb if f else s_xra, i)
                    for c in range(4):
                        k = 4 * f + c
                        mm = nc.tensor.transpose(PS[:, 6 + f, c * n:(c + 1) * n],
                                                 xt[0:n, i, k * P:(k + 1) * P], ident[0:n, 0:n])
                    mm.then_inc(s_xt, 1)
            pe.wait_ge(s_pad, 2)
            stat(0)

            k3 = [khh[:, hd, :].rearrange("p (r c) -> p r c", c=COLS) for hd in range(2)]
            l3 = [kll[:, hd, :].rearrange("p (r c) -> p r c", c=COLS) for hd in range(2)]
            with pe.Fori(0, NPAIR) as p:
                g = 3 * p + G_NA
                dense(6 * p, D0, uhc, ulc, g)
                pe.wait_ge(s_ob, 6 * p)
                dense(6 * p + 2, D1, uhc, ulc, g + 0)
                dense(6 * p + 4, D0, uhc, ulc, g + 1)

                def scores(u):
                    hd, v = u // 9, u % 9
                    pe.wait_ge(s_sb, TILES * p + max(u - 1, 0))
                    for i, k in enumerate((k3[hd], l3[hd])):
                        if v < 8:
                            j, x = v // 2, v % 2
                            mm = nc.tensor.matmul(PS[:, 6 + u % 2, 0:SN], qs[:, hd, P * v:P * v + P],
                                                  k[:, 5 * x:5 * x + WR + 1, K0[j]:K0[j] + WC],
                                                  start=(i == 0), stop=(i == 1))
                        else:
                            mm = nc.tensor.matmul(PS[:, 6 + u % 2, 0:WC], qs[:, hd, GRID:GRID + P],
                                                  k[:, 0, 0:WC], start=(i == 0), stop=(i == 1))
                    mm.then_inc(s_s, 1)

                def fill(f, tiles):
                    pe.wait_ge(s_tl, FILLS * p + max(f - 1, 0))
                    for c, t in enumerate(tiles):
                        mm = nc.tensor.transpose(PS[:, 3 + f % 2, P * c:P * c + P], t, ident[:, :])
                    mm.then_inc(s_tf, 1)

                def probs(u):
                    v = u % 9
                    pe.wait_ge(s_pr, TILES * p + (u + 1))
                    if v == 8:
                        at_ = [0]
                    elif v % 2:
                        at_ = [384, 0, 128, 256]
                    else:
                        at_ = [WC, WC + 128, WC + 256, 0]
                    fill(6 + u, [pb[:, u % 3, a:a + P] for a in at_])

                def pv(i):
                    hd, v = i // 5, i % 5
                    last_u = 9 * hd + (2 * v + 1 if v < 4 else 8)
                    pe.wait_ge(s_tl, FILLS * p + (7 + last_u))
                    if v in (0, 2, 4):
                        pe.wait_ge(s_ob, 6 * p + (3 * hd + v // 2))
                    if v == 4:
                        for i2, t in enumerate((pmh, pml)):
                            mm = nc.tensor.matmul(PS[:, 5, 0:P], vst[:, 16, hd, :], t[:, :],
                                                  start=(i2 == 0), stop=(i2 == 1))
                        mm.then_inc(s_pv, 1)
                        return
                    o0 = 256 * (v % 2)
                    sl = (4 * hd + v) % 2
                    for i2, t in enumerate((pth, ptl)):
                        parts = [(4 * v + 1, 1, 0, 256), (4 * v + 2, 2, 0, 256), (4 * v, 0, 0, 128),
                                 (4 * v + 3, 3, 128, 256), (16 + v % 2, 3, 0, 128), (16 + v % 2, 0, 128, 256)]
                        for i3, (tile, idx, a, b) in enumerate(parts):
                            mm = nc.tensor.matmul(PS[:, 5, o0 + a:o0 + b], vst[:, tile, hd, :],
                                                  t[:, sl, idx, a:b], start=(i2 == 0 and i3 == 0),
                                                  stop=(i2 == 1 and i3 == 5), skip_group_check=True)
                    mm.then_inc(s_pv, 1)

                pe.wait_ge(s_qlo, 2 * p + 2)
                pe.wait_ge(s_klc, 2 * p + 2)
                scores(0)
                scores(1)
                pe.wait_ge(s_vs, 12 * p + 12)
                pe.wait_ge(s_df, g + 3)
                for f in range(6):
                    fill(f, [vt[:, 3 * f + c, :] for c in range(3)])
                due = {9 * hd + (2 * v + 1 if v < 4 else 8) + 1: 5 * hd + v for hd in range(2) for v in range(5)}
                for u in range(TILES):
                    probs(u)
                    if u + 2 < TILES:
                        scores(u + 2)
                    if u in due:
                        pv(due[u])
                pv(9)
            proj_out(0)
            stat(1)
            ffn(0)
            stat(2)

            pe.wait_ge(s_gc, 16 * 7)
            pe.wait_ge(s_gz, CLEARS)
            with pe.Fori(0, NG) as g:
                gr = GGR * g + G_GQ
                for c, (set_, need) in enumerate(((D0, 0), (D1, 0), (D0, 1))):
                    if c == 0:
                        pe.wait_ge(s_gob, NQB * g)
                    dense(6 * g + (U_GQ + 2 * c), set_, uhc, ulc, gr + need)
                pe.wait_ge(s_df, gr + 3)
                for t in range(KT):
                    mm = nc.tensor.transpose(PS[:, D1 + t // 3, P * (t % 3):P * (t % 3) + P],
                                             tkv[:, P * t:P * t + P], ident[:, :])
                mm.then_inc(s_ga, 1)
                pe.wait_ge(s_gsq, 3 * g + 3)
                for i, x in enumerate((tn[:, 0, :], tn[:, 1, :], tn[:, 2, :])):
                    for c in range(NB):
                        mm = nc.tensor.matmul(PS[:, D0 + c, 0:CW], selb[:, i, :], x[:, c * CW:(c + 1) * CW],
                                              start=(i == 0), stop=(i == 2))
                mm.then_inc(s_ga, 1)
                pe.wait_ge(s_grc, g + 1)
                for i, c in enumerate((2, 0, 1)):
                    pe.wait_ge(s_df, gr + (4 + 2 * i))
                    spread(D1, bcb[:, c, :], ssq[:, :]).then_inc(s_ga, 1)
                    pe.wait_ge(s_df, gr + (6 + 2 * i))
                    spread(D0, rotb[:, :], tn[:, c, :]).then_inc(s_ga, 1)

                def cols(b):
                    return slice(QB * b, QB * b + (QB if b < 8 else P))

                def tile_max(b, i):
                    t = 4 * b + i
                    pe.wait_ge(s_mr, MT * g + t)
                    for c, k0 in enumerate((0, CW, T - CW)):
                        mm = nc.tensor.matmul(PS[:, c, 0:CW], qh[:, P * t:P * t + P], ks[:, k0:k0 + CW],
                                              start=True, stop=True)
                    mm.then_inc(s_mx, 1)

                def max_row(b):
                    nt = 4 if b < 8 else 1
                    pe.wait_ge(s_dg, MT * g + (4 * b + nt))
                    pe.wait_ge(s_gob, NQB * g + max(b - 1, 0))
                    for i in range(nt):
                        mm = nc.tensor.matmul(PS[:, 4, P * i:P * i + P], ones_r[:, :], dgm[:, i, :],
                                              start=True, stop=True)
                    mm.then_inc(s_mrow, 1)

                def sums(b):
                    nt = 4 if b < 8 else 1
                    pe.wait_ge(s_gacc, 8 * NQB * g + 8 * (b + 1))
                    pe.wait_ge(s_mset, NQB * g + min(b + 2, NQB))
                    for i in range(nt):
                        mm = nc.tensor.matmul(PS[:, 4, i:i + 1], acc[:, b % 2, P * i:P * i + P], ones[:, 0:1],
                                              start=True, stop=True)
                    mm.then_inc(s_gsum, 1)

                def sums_row(b):
                    nt = 4 if b < 8 else 1
                    pe.wait_ge(s_gdr, NQB * g + (b + 1))
                    for i in range(nt):
                        mm = nc.tensor.matmul(PS[:, 4, P * i:P * i + P], ones[:, :], dgs[:, i, :],
                                              start=True, stop=True)
                    mm.then_inc(s_gspr, 1)

                pe.wait_ge(s_gql, 5 * g + 5)
                pe.wait_ge(s_gqh, 5 * g + 5)
                for i in range(4):
                    tile_max(0, i)
                max_row(0)
                LAG = 3
                for s in range(STEPS + LAG):
                    b, kt = divmod(s, KT)
                    if s < STEPS:
                        if kt == 0:
                            pe.wait_ge(s_mset, NQB * g + (b + 1))
                        pe.wait_ge(s_gex, STEPS * g + max(s - 1, 0))
                        n = QB if b < 8 else P
                        for i, (k, q) in enumerate(((ks, qh), (kx, qx))):
                            mm = nc.tensor.matmul(PS[:, 6 + s % 2, 0:n], k[:, P * kt:P * kt + P], q[:, cols(b)],
                                                  start=(i == 0), stop=(i == 1))
                        mm.then_inc(s_sc, 1)
                        if b < 8 and kt in (0, 2, 4, 6) and kt // 2 < (4 if b < 7 else 1):
                            tile_max(b + 1, kt // 2)
                        if b < 8 and kt == 8:
                            max_row(b + 1)
                    if s >= LAG:
                        b2, kt2 = divmod(s - LAG, KT)
                        n = QB if b2 < 8 else P
                        pe.wait_ge(s_gpl, STEPS * g + (s - LAG + 1))
                        if kt2 == 0:
                            pe.wait_ge(s_gob, NQB * g + max(b2 - 1, 0))
                        for i, t in enumerate((ph, pl)):
                            mm = nc.tensor.matmul(PS[:, OB[b2 % 2], 0:n], vg[:, kt2, :], t[:, (s - LAG) % 3, 0:n],
                                                  start=(kt2 == 0 and i == 0), stop=(kt2 == 8 and i == 1))
                        mm.then_inc(s_gpv, 1)
                        if kt2 == 8:
                            sums(b2)
                        if b2 and kt2 == 0:
                            sums_row(b2 - 1)
                sums_row(NQB - 1)
            proj_out(1)
            stat(3)
            ffn(1)
            stat(4)
            for i in range(8):
                pe.wait_ge(s_fs, KC)
                for f in range(2):
                    if i:
                        pe.wait_ge(s_fcb if f else s_fca, i)
                    for c in range(4):
                        mm = nc.tensor.transpose(PS[:, 6 + f, P * c:P * c + P],
                                                 h[:, 4 * f + c, P * i:P * i + P], ident[:, :])
                    mm.then_inc(s_ft, 1)

        @block.scalar
        def _(act):
            def squares(k, m, buf, sem_, need):
                act.wait_ge(sem_, need)
                if m >= 2:
                    act.wait_ge(s_acc, (KC - 1) * k + m - 1)
                nc.scalar.activation(buf[:, m % 2, :], h[:, m, :], ACT.Square).then_inc(s_sq, 1)
                if k < 4:
                    nc.scalar.activation(uh[:, m, :], h[:, m, :], ACT.Copy,
                                         scale=gains[:, k, m:m + 1]).then_inc(s_uh, 1)

            def root(k):
                act.wait_ge(s_df, G_ST[k] + 1)
                nc.scalar.activation(rstd[:, :], rstd[:, :], ACT.Sqrt).then_inc(s_rt, 1)

            def ffn(l):
                gb = G_FF[l]

                def up(g, par):
                    for b in range(2):
                        act.wait_ge(s_df, g + (2 * b + 1))
                        nc.scalar.activation(at[:, b, :], at[:, b, :], ACT.Silu).then_inc(s_silu, 1)
                        act.wait_ge(s_df, g + (2 * b + 2))
                        nc.scalar.activation(gh[:, par, b, :], at[:, b, :], ACT.Copy).then_inc(s_gh, 1)

                up(gb, 0)
                with act.Fori(0, FIT // 2) as i:
                    for s in range(2):
                        up(24 * i + (gb + 4 + 12 * s), 1 - s)
                for m in range(KC):
                    squares(2 * l + 2, m, sq_ffn, s_df, gb + 125 + m)
                root(2 * l + 2)

            def spill_h(l):
                act.wait_ge(s_ur, KC * (2 * l + 1))
                for m in range(KC):
                    act.dma_start(h_spill[:, m, :], h[:, m, :]).then_inc(s_hsp, 16)
                act.wait_ge(s_hsp, 16 * KC * (l + 1))

            def proj_out(l):
                act.wait_ge(s_osp, 16 * (KC + NG * l))
                for m in range(KC):
                    act.dma_start(h[:, m, :], h_spill[:, m, :]).then_inc(s_hld, 16)
                for m in range(2):
                    act.dma_start(oraw[:, m, :], o_spill[:, m, :]).then_inc(s_old, 16)
                for m in range(KC):
                    act.wait_ge(s_old, 16 * (KC * l + min(m + 2, KC)))
                    nc.scalar.activation(oh[:, m, :], oraw[:, m % 2, :], ACT.Copy).then_inc(s_oh, 1)
                    if m + 2 < KC:
                        act.wait_ge(s_or, KC * l + m + 1)
                        act.dma_start(oraw[:, m % 2, :], o_spill[:, m + 2, :]).then_inc(s_old, 16)
                for m in range(KC):
                    squares(2 * l + 1, m, sq_wo, s_df, G_WO[l] + m + 1)
                root(2 * l + 1)

            act.dma_start(gains[:, 0, :], A["norm_mix"][0].rearrange("(k p) -> p k", p=P),
                          allow_slow_non_contiguous=True).then_inc(s_const, 16)
            act.dma_start(gains[:, 1, :], A["norm_ffn"][0].rearrange("(k p) -> p k", p=P),
                          allow_slow_non_contiguous=True).then_inc(s_const, 16)
            act.dma_start(gains[:, 2, :], A["norm_mix"][1].rearrange("(k p) -> p k", p=P),
                          allow_slow_non_contiguous=True).then_inc(s_const, 16)
            act.dma_start(gains[:, 3, :], A["norm_ffn"][1].rearrange("(k p) -> p k", p=P),
                          allow_slow_non_contiguous=True).then_inc(s_const, 16)
            act.dma_start(gains[:, 4, :], A["norm_final"].rearrange("(k p) -> p k", p=P),
                          allow_slow_non_contiguous=True).then_inc(s_const, 16)
            for i in range(9):
                n = P if i < 8 else META
                act.wait_ge(s_xt, 2 * i + 2)
                nc.scalar.activation(h[:, 4:8, P * i:P * i + n],
                                     PS[:, 7, 0:4 * n].rearrange("p (c n) -> p c n", n=n),
                                     ACT.Copy).then_inc(s_xrb, 1)
            act.wait_ge(s_const, 80)
            act.wait_ge(s_pad, 2)
            act.wait_ge(s_xrb, 9)
            for m in range(KC):
                squares(0, m, sq_in, s_xra, 9)
            root(0)
            spill_h(0)

            act.dma_start(maskb[:, :, :, :], C["mask"]).then_inc(s_na, 16)
            act.dma_start(mb_raw[:, :], A["a_meta_bias"].rearrange("a h m -> a (h m)")
                          .partition_broadcast(P)).then_inc(s_na, 16)
            act.wait_ge(s_zero, 6)
            act.dma_start(bias_rows.rearrange("h c a e -> (h c a e)").rearrange("(p n) -> p n", p=P),
                          vt[:, :, :].rearrange("p a b -> p (a b)")[:, 0:NH * CB * ARR * EW // P]
                          ).then_inc(s_bfill, 16)
            act.wait_ge(s_bfill, 16)
            for c in range(CB):
                act.dma_start(bias_rows[:, c, 4:19, c + 1:c + 32], A["a_rel_bias"][0],
                              allow_slow_non_contiguous=True).then_inc(s_brow, 16)
            act.wait_ge(s_brow, 16 * CB)
            with act.Fori(0, NPAIR) as p:
                act.wait_ge(s_bm, 34 * p)
                for hd in range(2):
                    for x in range(2):
                        for r in range(HR):
                            a0 = (7 if x else 11) - r
                            act.dma_start(
                                biasb[CB * r:CB * r + CB, hd, x, :].rearrange("p (a e) -> p a e", e=EW),
                                bias_rows[bass.ds(2 * p + hd, 1), :, a0:a0 + WR, :]
                                .rearrange("h c a e -> (h c) a e")).then_inc(s_bload[hd], 16)
                g = 3 * p + G_NA
                act.wait_ge(s_df, g + 1)
                act.wait_ge(s_s, TILES * p)
                for hd in range(2):
                    r = slice(64 * hd, 64 * hd + 64)
                    nc.scalar.activation(qs[r, hd, 0:TP], ssq[r, :], ACT.Copy).then_inc(s_qhi, 1)
                act.wait_ge(s_df, g + 2)
                grid = keys[:, COLS:COLS + GRID].rearrange("p (r j c) -> p r j c", j=NJ, c=CB)
                nc.scalar.activation(grid, ssq[:, 0:GRID].rearrange("p (j r c) -> p r j c", j=NJ, c=CB),
                                     ACT.Copy).then_inc(s_kn, 1)
                for row in (0, ROWS + 1):
                    for c0 in (8, 32):
                        nc.scalar.activation(keys[:, COLS * row + c0:COLS * row + c0 + META],
                                             ssq[:, GRID:T], ACT.Copy).then_inc(s_kn, 1)
                act.wait_ge(s_kn, 5 * p + 5)
                for hd in range(2):
                    for half in (hd, 1 - hd):
                        nc.scalar.activation(khh[64 * half:64 * half + 64, hd, :],
                                             keys[64 * hd:64 * hd + 64, :], ACT.Copy).then_inc(s_khi, 1)
                for hd in range(2):
                    act.wait_ge(s_klo, 2 * p + (hd + 1))
                    nc.scalar.activation(kll[64 * (1 - hd):64 * (1 - hd) + 64, hd, :],
                                         kll[64 * hd:64 * hd + 64, hd, :], ACT.Copy).then_inc(s_klc, 1)

                def exp(u):
                    w = SN if u % 9 < 8 else WC
                    act.wait_ge(s_sb, TILES * p + (u + 1))
                    nc.scalar.activation(pb[:, u % 3, 0:w], pb[:, u % 3, 0:w], ACT.Exp,
                                         bias=small[:, u % 3, 0:1], scale=-1.0,
                                         accum_out=small[:, u % 3, 1:2]).then_inc(s_ex, 1)

                def t_hi(u):
                    hd, v = u // 9, u % 9
                    act.wait_ge(s_tf, FILLS * p + (u + 7))
                    bank = 3 + u % 2
                    if v == 8:
                        act.wait_ge(s_pv, 10 * p + 5 * hd)
                        nc.scalar.activation(pmh[:, :], PS[:, bank, 0:P], ACT.Copy).then_inc(s_th, 1)
                        return
                    st_ = 4 * hd + v // 2
                    act.wait_ge(s_pv, 10 * p + (5 * ((st_ - 2) // 4) + (st_ - 2) % 4 + 1 if st_ >= 2 else 0))
                    x = v % 2
                    nc.scalar.activation(pth[:, st_ % 2, :, P * x:P * x + P],
                                         PS[:, bank, :].rearrange("p (c n) -> p c n", n=P),
                                         ACT.Copy).then_inc(s_th, 1)

                def o_part(i):
                    act.wait_ge(s_pv, 10 * p + (5 * (i // 3) + (2, 4, 5)[i % 3]))
                    act.wait_ge(s_ob, 6 * p + i)
                    n = 512 if i % 3 < 2 else META
                    nc.scalar.activation(otmp[:, 0:n], PS[64:128, 5, 0:n], ACT.Copy).then_inc(s_oa, 1)

                exp(0)
                exp(1)
                for f in range(6):
                    act.wait_ge(s_tf, FILLS * p + (f + 1))
                    act.wait_ge(s_pv, 10 * p)
                    nc.scalar.activation(
                        vst[:, 3 * f:3 * f + 3, :, 0:HD],
                        PS[:, 3 + f % 2, 0:3 * P].rearrange("p (t h d) -> p t h d", t=3, h=2),
                        ACT.Copy).then_inc(s_th, 1)
                o_due = {5: 0, 9: 1, 10: 2, 14: 3}
                for u in range(TILES):
                    t_hi(u)
                    if u + 2 < TILES:
                        exp(u + 2)
                    if u in o_due:
                        o_part(o_due[u])
                o_part(4)
                o_part(5)
                act.wait_ge(s_ob, 6 * p + 6)
                act.dma_start(o_spill[:, bass.ds(p, 1), :].rearrange("p a t -> p (a t)"), ob[:, :]).then_inc(s_osp, 16)
            proj_out(0)
            ffn(0)
            spill_h(1)

            for dst, name in ((cosb[:, :], "cos"), (sinb[:, :], "sin"), (selb[:, :, :], "sel"),
                              (bcb[:, :, :], "bc"), (rotb[:, :], "rot")):
                act.dma_start(dst, C[name]).then_inc(s_gc, 16)
            for e in range(2):
                act.dma_start(gnb[64 * e:64 * e + 64, 0:1], A["b_q_norm"].rearrange("a (d b) -> (a d) b", b=1)).then_inc(s_gc, 16)
            act.dma_start(gnb[0:64, 1:2], A["b_k_norm"].rearrange("a (d b) -> (a d) b", b=1)).then_inc(s_gc2, 16)
            with act.Fori(0, NG) as g:
                gr = GGR * g + G_GQ
                if True:
                    for c in range(3):
                        act.wait_ge(s_df, gr + (c + 1))
                        src = tq[:, c, :] if c < 2 else tkv[:, 0:TP]
                        nc.scalar.activation(tn[:, c, :], src, ACT.Square).then_inc(s_gsq, 1)
                act.wait_ge(s_ga, 8 * g + 1)
                nc.scalar.activation(
                    vg[:, :, 0:HD].rearrange("p (b t) d -> p b t d", b=3),
                    PS[:, D1:D1 + 3, 0:3 * P].rearrange("p b (t d) -> p b t d", t=3)[:, :, :, HD:P],
                    ACT.Copy).then_inc(s_vgh, 1)
                act.wait_ge(s_df, gr + 5)
                nc.scalar.activation(ssq[:, :], ssq[:, :], ACT.Sqrt).then_inc(s_gsr, 1)
                act.wait_ge(s_rot, 3 * g + 1)
                nc.scalar.activation(ks[0:64, 0:TP], tkv[0:64, 0:TP], ACT.Copy).then_inc(s_gs1, 1)
                nc.scalar.activation(kx[0:64, 0:T], tkv[0:64, 0:T], ACT.Copy).then_inc(s_gqh, 1)
                for hh in range(GH):
                    c, e = divmod(hh, 2)
                    act.wait_ge(s_rot, 3 * g + (2 + c))
                    src = tq[64 * e:64 * e + 64, c, :]
                    for half in range(2):
                        q = slice(64 * half, 64 * half + 64)
                        nc.scalar.activation(qh[q, GH * GRID + META * hh:GH * GRID + META * hh + META],
                                             src[:, GRID:T], ACT.Copy).then_inc(s_gs1, 1)
                        nc.scalar.activation(qh[q, GRID * hh:GRID * hh + GRID], src[:, 0:GRID],
                                             ACT.Copy).then_inc(s_gs1 if half == 0 else s_gqh, 1)

                def set_max(b):
                    n = QB if b < 8 else P
                    act.wait_ge(s_mrow, NQB * g + (b + 1))
                    nc.scalar.activation(qx[64:65, QB * b:QB * b + n], PS[64:65, 4, 0:n],
                                         ACT.Copy).then_inc(s_mset, 1)

                act.wait_ge(s_gql, 5 * g + 5)
                set_max(0)
                for s in range(STEPS):
                    b, kt = divmod(s, KT)
                    n = QB if b < 8 else P
                    act.wait_ge(s_sc, STEPS * g + (s + 1))
                    if s >= 3:
                        b3, k3_ = divmod(s - 3, KT)
                        act.wait_ge(s_gpl, STEPS * g + (s - 2))
                        act.wait_ge(s_gacc, 8 * NQB * g + (8 * b3 + max(k3_, 1)))
                    q = slice(0, META) if kt == KT - 1 else slice(0, P)
                    nc.scalar.activation(pf[q, s % 3, 0:n], PS[q, 6 + s % 2, 0:n], ACT.Exp).then_inc(s_gex, 1)
                    act.wait_ge(s_gex, STEPS * g + (s + 1))
                    if s >= 3:
                        act.wait_ge(s_gpv, STEPS * g + (s - 2))
                    nc.scalar.activation(ph[:, s % 3, 0:n], pf[:, s % 3, 0:n], ACT.Copy).then_inc(s_gph, 1)
                    if b < 8 and kt == 8:
                        set_max(b + 1)
                    if b and kt == 4:
                        act.wait_ge(s_gpv, STEPS * g + KT * b)
                        act.wait_ge(s_gob, NQB * g + (b - 1))
                        nc.scalar.activation(ot1[:, :], PS[64:128, OB[(b - 1) % 2], :], ACT.Copy).then_inc(s_goa, 1)
                act.wait_ge(s_gpv, STEPS * g + STEPS)
                act.wait_ge(s_gob, NQB * g + 8)
                nc.scalar.activation(ot1[:, 0:P], PS[64:128, OB[0], 0:P], ACT.Copy).then_inc(s_goa, 1)
                act.wait_ge(s_gob, NQB * g + 9)
                act.dma_start(o_spill[:, bass.ds(2 * g, 2), :], ob2[:, :, :]).then_inc(s_osp, 16)
            proj_out(1)
            ffn(1)
            for i in range(8):
                act.wait_ge(s_ft, 2 * i + 1)
                if i >= 2:
                    act.wait_ge(s_out[i % 2], 16 * HR * (i // 2))
                nc.scalar.activation(fin[:, i % 2, 0:512], PS[:, 6, :], ACT.Copy).then_inc(s_fca, 1)

        @block.vector
        def _(dve):
            def add_square(k, m, buf):
                dve.wait_ge(s_sq, KC * k + m + 1)
                if m == 0:
                    ins = nc.vector.tensor_copy(ssq[:, :], buf[:, 0, :])
                else:
                    dve.wait_ge(s_acc, (KC - 1) * k + m)
                    ins = nc.vector.tensor_tensor(ssq[:, :], ssq[:, :], buf[:, m % 2, :], ALU.add)
                ins.then_inc(s_ssq if m == KC - 1 else s_acc, 1)
                if k < 4:
                    dve.wait_ge(s_uh, KC * k + m + 1)
                    nc.vector.scalar_tensor_tensor(ul[:, m, :], h[:, m, :], gains[:, k, m:m + 1],
                                                   uh[:, m, :].bitcast(F32), op0=ALU.mult,
                                                   op1=ALU.subtract).then_inc(s_ur, 1)

            def rsqrt(k):
                dve.wait_ge(s_st, k + 1)
                nc.vector.tensor_scalar(banks(rstd[:, :]), PS[:, D1:D1 + NB, 0:CW], 1.0 / D, EPS,
                                        ALU.mult, ALU.add).then_inc(s_df, 1)
                dve.wait_ge(s_rt, k + 1)
                nc.vector.reciprocal(rstd[:, :], rstd[:, :]).then_inc(s_rs, 1)
                dve.wait_ge(s_rs, k + 1)

            def add_to_h(m, set_, need_sem, need, inc=True):
                dve.wait_ge(need_sem, need)
                hm = banks(h[:, m, :])
                nc.vector.tensor_tensor(hm, PS[:, set_:set_ + NB, 0:CW], hm, ALU.add).then_inc(s_df, 1)

            def ffn(l):
                ub, gb = U_FF[l], G_FF[l]

                def up(n, g, k, par):
                    for b in range(2):
                        a3 = banks(at[:, b, :])
                        dve.wait_ge(s_un, n + (4 * b + 2))
                        dve.wait_ge(s_gr, k + b)
                        nc.vector.tensor_tensor(a3, PS[:, D0:D0 + NB, 0:CW], banks(rstd[:, :]),
                                                ALU.mult).then_inc(s_df, 1)
                        dve.wait_ge(s_silu, k + (b + 1))
                        nc.vector.tensor_tensor(at[:, b, :], at[:, b, :], rstd[:, :], ALU.mult).then_inc(s_sr, 1)
                        dve.wait_ge(s_sr, k + (b + 1))
                        dve.wait_ge(s_un, n + (4 * b + 4))
                        nc.vector.tensor_tensor(a3, PS[:, D1:D1 + NB, 0:CW], a3, ALU.mult).then_inc(s_df, 1)
                        dve.wait_ge(s_gh, k + (b + 1))
                        nc.vector.tensor_tensor(gl[:, par, b, :], at[:, b, :], gh[:, par, b, :].bitcast(F32),
                                                ALU.subtract).then_inc(s_gr, 1)

                def down(n, g):
                    for m in range(KC):
                        if m == 0:
                            dve.wait_ge(s_df, g)
                        add_to_h(m, D1 if m % 2 else D0, s_un, n + (m + 1))

                k0 = 2 * FIT * l
                up(ub, gb, k0, 0)
                with dve.Fori(0, FIT // 2) as i:
                    for s in range(2):
                        up(32 * i + (ub + 8 + 16 * s), None, 4 * i + (k0 + 2 + 2 * s), 1 - s)
                        down(32 * i + (ub + 16 + 16 * s), 24 * i + (gb + 8 + 12 * s))
                k = 2 * l + 2
                dve.wait_ge(s_df, gb + 124)
                for m in range(KC):
                    add_to_h(m, D1 if m % 2 else D0, s_un, ub + 168 + m + 1)
                    if m:
                        add_square(k, m - 1, sq_ffn)
                add_square(k, KC - 1, sq_ffn)
                rsqrt(k)

            def proj_out(l):
                for m in range(KC):
                    dve.wait_ge(s_oh, KC * l + m + 1)
                    nc.vector.tensor_tensor(ol[:, m, :], oraw[:, m % 2, :], oh[:, m, :].bitcast(F32),
                                            ALU.subtract).then_inc(s_or, 1)
                dve.wait_ge(s_hld, 16 * KC * (l + 1))
                for m in range(KC):
                    add_to_h(m, D1 if m % 2 else D0, s_un, U_WO[l] + 2 * m + 2)
                    if m:
                        add_square(2 * l + 1, m - 1, sq_wo)
                add_square(2 * l + 1, KC - 1, sq_wo)
                rsqrt(2 * l + 1)

            nc.vector.memset(ones[:, :], 1.0).then_inc(s_pad, 1)
            nc.vector.memset(h[:, :, T:TP], 0.0).then_inc(s_pad, 1)
            for i in range(9):
                n = P if i < 8 else META
                dve.wait_ge(s_xt, 2 * i + 1)
                nc.vector.tensor_copy(h[:, 0:4, P * i:P * i + n],
                                      PS[:, 6, 0:4 * n].rearrange("p (c n) -> p c n", n=n)).then_inc(s_xra, 1)
            dve.wait_ge(s_const, 80)
            dve.wait_ge(s_pad, 2)
            dve.wait_ge(s_xra, 9)
            for m in range(KC):
                add_square(0, m, sq_in)
            rsqrt(0)

            dve.wait_ge(s_zero, 6)
            dve.wait_ge(s_na, 32)
            for cls, at_ in ((0, 8), (1, 0)):
                nc.vector.tensor_scalar(mbn[:, :, cls, at_:at_ + META],
                                        mb_raw[:, :].rearrange("p (h m) -> p h m", m=META), -1.0, None,
                                        ALU.mult).then_inc(s_mbn, 1)
            with dve.Fori(0, NPAIR) as p:
                g = 3 * p + G_NA
                dve.wait_ge(s_un, 6 * p + 2)
                dve.wait_ge(s_klo, 2 * p)
                nc.vector.scalar_tensor_tensor(banks(ssq[:, :]), PS[:, D0:D0 + NB, 0:CW], -HD ** -0.5,
                                               banks(rstd[:, :]), op0=ALU.mult, op1=ALU.mult).then_inc(s_df, 1)
                for hd in range(2):
                    r = slice(64 * hd, 64 * hd + 64)
                    r2 = slice(64 - 64 * hd, 128 - 64 * hd)
                    dve.wait_ge(s_qhi, 2 * p + (hd + 1))
                    nc.vector.tensor_tensor(qs[r2, hd, 0:TP], ssq[r, :], qs[r, hd, 0:TP].bitcast(F32),
                                            ALU.subtract).then_inc(s_qlo, 1)
                dve.wait_ge(s_un, 6 * p + 4)
                dve.wait_ge(s_qlo, 2 * p + 2)
                nc.vector.tensor_tensor(banks(ssq[:, :]), PS[:, D1:D1 + NB, 0:CW], banks(rstd[:, :]),
                                        ALU.mult).then_inc(s_df, 1)
                for hd in range(2):
                    r = slice(64 * hd, 64 * hd + 64)
                    dve.wait_ge(s_khi, 4 * p + (2 * hd + 1))
                    nc.vector.tensor_tensor(kll[r, hd, :], keys[r, :], khh[r, hd, :].bitcast(F32),
                                            ALU.subtract).then_inc(s_klo, 1)
                dve.wait_ge(s_un, 6 * p + 6)
                dve.wait_ge(s_vs, 12 * p)
                nc.vector.tensor_tensor(banks(vals[:, :]), PS[:, D0:D0 + NB, 0:CW], banks(rstd[:, :]),
                                        ALU.mult).then_inc(s_df, 1)

                def bias(u):
                    w = SN if u % 9 < 8 else WC
                    dve.wait_ge(s_s, TILES * p + (u + 1))
                    dve.wait_ge(s_bm, 34 * p + (2 * (u + 1) - (u >= 8) - (u >= 17)))
                    dve.wait_ge(s_tf, FILLS * p + max(u + 4, 0) if u >= 3 else FILLS * p)
                    nc.vector.memset(small[:, u % 3, 3:4], 0.0).then_inc(s_car, 1)
                    nc.vector.tensor_tensor_reduce(pb[:, u % 3, 0:w], PS[:, 6 + u % 2, 0:w], bm[:, u % 3, 0:w],
                                                   1.0, 3e38, ALU.add, ALU.min,
                                                   small[:, u % 3, 0:1]).then_inc(s_sb, 1)

                def norm(u):
                    w = SN if u % 9 < 8 else WC
                    dve.wait_ge(s_ex, TILES * p + (u + 1))
                    nc.vector.reciprocal(small[:, u % 3, 2:3], small[:, u % 3, 1:2]).then_inc(s_dv, 1)
                    dve.wait_ge(s_dv, TILES * p + (u + 1))
                    nc.vector.tensor_scalar(pb[:, u % 3, 0:w], pb[:, u % 3, 0:w], small[:, u % 3, 2:3], None,
                                            ALU.mult).then_inc(s_pr, 1)

                def t_lo(u):
                    hd, v = u // 9, u % 9
                    bank = 3 + u % 2
                    dve.wait_ge(s_th, FILLS * p + (u + 7))
                    if v == 8:
                        nc.vector.tensor_tensor(pml[:, :], PS[:, bank, 0:P], pmh[:, :].bitcast(F32),
                                                ALU.subtract).then_inc(s_tl, 1)
                        return
                    st_, x = 4 * hd + v // 2, v % 2
                    nc.vector.tensor_tensor(ptl[:, st_ % 2, :, P * x:P * x + P],
                                            PS[:, bank, :].rearrange("p (c n) -> p c n", n=P),
                                            pth[:, st_ % 2, :, P * x:P * x + P].bitcast(F32),
                                            ALU.subtract).then_inc(s_tl, 1)

                def o_sum(i):
                    hd, w = i // 3, i % 3
                    n = 512 if w < 2 else META
                    dve.wait_ge(s_oa, 6 * p + (i + 1))
                    dve.wait_ge(s_osp, 16 * p)
                    nc.vector.tensor_tensor(ob[64 * hd:64 * hd + 64, 512 * w:512 * w + n], PS[0:64, 5, 0:n],
                                            otmp[:, 0:n], ALU.add).then_inc(s_ob, 1)

                bias(0)
                norm(0)
                bias(1)
                norm(1)
                for f in range(6):
                    dve.wait_ge(s_th, FILLS * p + (f + 1))
                    nc.vector.tensor_tensor(
                        vst[:, 3 * f:3 * f + 3, :, HD:P],
                        PS[:, 3 + f % 2, 0:3 * P].rearrange("p (t h d) -> p t h d", t=3, h=2),
                        vst[:, 3 * f:3 * f + 3, :, 0:HD].bitcast(F32), ALU.subtract).then_inc(s_tl, 1)
                o_due = {5: 0, 9: 1, 10: 2, 14: 3}
                for u in range(TILES):
                    if u + 2 < TILES:
                        bias(u + 2)
                    t_lo(u)
                    if u + 2 < TILES:
                        norm(u + 2)
                    if u in o_due:
                        o_sum(o_due[u])
                o_sum(4)
                o_sum(5)
            proj_out(0)
            ffn(0)

            dve.wait_ge(s_hsp, 16 * KC * 2)
            dve.wait_ge(s_gmem, 2)
            zero = ob2[:, :, :].rearrange("p a t -> p (a t)")
            m0 = GH * GRID + GH * META
            clear = [qh[:, m0:QW], qx[0:64, m0:QW], ks[:, TP:TW], kx[0:64, T:TW], kx[64:P, :]]
            clear += [qx[64:P, a:min(a + 2 * TP, QW)] for a in range(0, QW, 2 * TP)]
            for t in clear:
                rows = slice(0, t.shape[0])
                nc.vector.tensor_copy(t, zero[rows, 0:t.shape[1]]).then_inc(s_gz, 1)
            nc.vector.tensor_copy(ones_r[:, :], ones[:, :]).then_inc(s_gz, 1)
            dve.wait_ge(s_gz, CLEARS - 1)
            nc.vector.tensor_scalar(kx[64:65, 0:T], zero[64:65, 0:T], 1.0, None, ALU.add).then_inc(s_gz, 1)
            dve.wait_ge(s_gc, 16 * 7)
            dve.wait_ge(s_gc2, 16)
            nc.vector.tensor_scalar(gnb[:, 0:1], gnb[:, 0:1], HD ** -0.5, None, ALU.mult).then_inc(s_gnb, 1)
            dve.wait_ge(s_gnb, 1)
            with dve.Fori(0, NG) as g:
                gr = GGR * g + G_GQ
                for c in range(3):
                    set_ = D1 if c == 1 else D0
                    dst = tq[:, c, :] if c < 2 else tkv[:, 0:TP]
                    dve.wait_ge(s_un, 6 * g + (U_GQ + 2 * c + 2))
                    nc.vector.tensor_tensor(banks(dst), PS[:, set_:set_ + NB, 0:CW], banks(rstd[:, :]),
                                            ALU.mult).then_inc(s_df, 1)
                dve.wait_ge(s_vgh, g + 1)
                nc.vector.tensor_tensor(
                    vg[:, :, HD:P].rearrange("p (b t) d -> p b t d", b=3),
                    PS[:, D1:D1 + 3, 0:3 * P].rearrange("p b (t d) -> p b t d", t=3)[:, :, :, HD:P],
                    vg[:, :, 0:HD].bitcast(F32).rearrange("p (b t) d -> p b t d", b=3),
                    ALU.subtract).then_inc(s_df, 1)
                dve.wait_ge(s_ga, 8 * g + 2)
                nc.vector.tensor_scalar(banks(ssq[:, :]), PS[:, D0:D0 + NB, 0:CW], 1.0 / HD, EPS,
                                        ALU.mult, ALU.add).then_inc(s_df, 1)
                dve.wait_ge(s_gsr, g + 1)
                nc.vector.reciprocal(ssq[:, :], ssq[:, :]).then_inc(s_grc, 1)
                for i, c in enumerate((2, 0, 1)):
                    q = slice(0, 64) if c == 2 else slice(0, P)
                    raw = tq[q, c, :] if c < 2 else tkv[q, 0:TP]
                    gain = gnb[q, 1:2] if c == 2 else gnb[q, 0:1]
                    dve.wait_ge(s_ga, 8 * g + (3 + 2 * i))
                    nc.vector.scalar_tensor_tensor(banks(tn[q, c, :]), banks(raw), gain,
                                                   PS[q, D1:D1 + NB, 0:CW], op0=ALU.mult,
                                                   op1=ALU.mult).then_inc(s_df, 1)
                    dve.wait_ge(s_df, gr + (6 + 2 * i))
                    nc.vector.tensor_tensor(raw, tn[q, c, :], cosb[q, :], ALU.mult).then_inc(s_cs, 1)
                    dve.wait_ge(s_ga, 8 * g + (4 + 2 * i))
                    dve.wait_ge(s_cs, 3 * g + (i + 1))
                    nc.vector.tensor_tensor(banks(tn[q, c, :]), PS[q, D0:D0 + NB, 0:CW], banks(sinb[q, :]),
                                            ALU.mult).then_inc(s_df, 1)
                    dve.wait_ge(s_df, gr + (7 + 2 * i))
                    nc.vector.tensor_tensor(raw, raw, tn[q, c, :], ALU.add).then_inc(s_rot, 1)
                dve.wait_ge(s_gqh, 5 * g + 1)
                nc.vector.tensor_tensor(ks[64:128, 0:TP], tkv[0:64, 0:TP], ks[0:64, 0:TP].bitcast(F32),
                                        ALU.subtract).then_inc(s_gql, 1)
                dve.wait_ge(s_rot, 3 * g + 3)
                for hh in range(GH):
                    c, e = divmod(hh, 2)
                    r = slice(64 * e, 64 * e + 64)
                    dve.wait_ge(s_gqh, 5 * g + (hh + 2))
                    m0 = GH * GRID + META * hh
                    nc.vector.tensor_tensor(qx[0:64, m0:m0 + META], tq[r, c, GRID:T],
                                            qh[r, m0:m0 + META].bitcast(F32), ALU.subtract).then_inc(s_gs2, 1)
                    nc.vector.tensor_tensor(qx[0:64, GRID * hh:GRID * hh + GRID], tq[r, c, 0:GRID],
                                            qh[r, GRID * hh:GRID * hh + GRID].bitcast(F32),
                                            ALU.subtract).then_inc(s_gql, 1)

                def take_max(b, i):
                    t = 4 * b + i
                    dve.wait_ge(s_mx, MT * g + (t + 1))
                    dve.wait_ge(s_mrow, NQB * g + b)
                    nc.vector.tensor_reduce(nmx[:, i:i + 1], PS[:, 0:3, 0:CW], AX.XY, ALU.max,
                                            negate=True).then_inc(s_mr, 1)
                    dve.wait_ge(s_mr, MT * g + (t + 1))
                    nc.vector.tensor_scalar(dgm[:, i, :], ident[:, :], nmx[:, i:i + 1], None,
                                            ALU.mult).then_inc(s_dg, 1)

                def divide(b):
                    nt = 4 if b < 8 else 1
                    dve.wait_ge(s_gsum, NQB * g + (b + 1))
                    nc.vector.reciprocal(rsm[:, 0:nt], PS[:, 4, 0:nt]).then_inc(s_rsm, 1)
                    dve.wait_ge(s_rsm, NQB * g + (b + 1))
                    for i in range(nt):
                        nc.vector.tensor_scalar(dgs[:, i, :], ident[:, :], rsm[:, i:i + 1], None,
                                                ALU.mult).then_inc(s_gdr if i == nt - 1 else s_gds, 1)

                def o_block(b):
                    n = QB if b < 8 else P
                    dve.wait_ge(s_goa, NQB * g + (b + 1))
                    dve.wait_ge(s_gspr, NQB * g + (b + 1))
                    nc.vector.tensor_tensor(ot1[:, 0:n], PS[0:64, OB[b % 2], 0:n], ot1[:, 0:n], ALU.add).then_inc(s_got, 1)
                    dve.wait_ge(s_got, NQB * g + (b + 1))
                    dve.wait_ge(s_osp, 16 * g + 16 * KC)
                    if b < 8:
                        hh, half = divmod(b, 2)
                        c, e = divmod(hh, 2)
                        nc.vector.tensor_tensor(ob2[64 * e:64 * e + 64, c, QB * half:QB * half + QB],
                                                ot1[:, :], PS[0:64, 4, :], ALU.mult).then_inc(s_gob, 1)
                        return
                    for hh in range(GH):
                        c, e = divmod(hh, 2)
                        m = slice(META * hh, META * hh + META)
                        nc.vector.tensor_tensor(ob2[64 * e:64 * e + 64, c, GRID:T], ot1[:, m],
                                                PS[0:64, 4, m], ALU.mult).then_inc(s_gob if hh == 3 else s_gs2, 1)

                for i in range(4):
                    take_max(0, i)
                for s in range(STEPS):
                    b, kt = divmod(s, KT)
                    n = QB if b < 8 else P
                    dve.wait_ge(s_gph, STEPS * g + (s + 1))
                    nc.vector.tensor_tensor(pl[:, s % 3, 0:n], pf[:, s % 3, 0:n], ph[:, s % 3, 0:n].bitcast(F32),
                                            ALU.subtract).then_inc(s_gpl, 1)
                    if b and kt == 2:
                        divide(b - 1)
                    if b and kt == 5:
                        o_block(b - 1)
                    if b < 8 and kt in (0, 2, 4, 6) and kt // 2 < (4 if b < 7 else 1):
                        take_max(b + 1, kt // 2)
                divide(8)
                o_block(8)
            proj_out(1)
            ffn(1)
            dve.wait_ge(s_rs, 5)
            for m in range(KC):
                nc.vector.scalar_tensor_tensor(h[:, m, :], h[:, m, :], gains[:, 4, m:m + 1], rstd[:, :],
                                               op0=ALU.mult, op1=ALU.mult).then_inc(s_fs, 1)
            for i in range(8):
                dve.wait_ge(s_ft, 2 * i + 2)
                if i >= 2:
                    dve.wait_ge(s_out[i % 2], 16 * HR * (i // 2))
                nc.vector.tensor_copy(fin[:, i % 2, 512:1024], PS[:, 7, :]).then_inc(s_fcb, 1)


def tables():
    q = np.arange(P)
    mask = np.zeros((P, 2, NJ, WR, WC), np.float32)
    for x in range(2):
        r = HR * x + q // CB
        kr = np.arange(WR) + 4 * x
        rs = np.clip(r - WIN_R // 2, 0, ROWS - WIN_R)
        row_ok = (kr >= rs[:, None]) & (kr < rs[:, None] + WIN_R)
        for j in range(NJ):
            c = CB * j + q % CB
            kc = np.arange(WC) + K0[j]
            cs = np.clip(c - WIN_C // 2, 0, COLS - WIN_C)
            col_ok = (kc >= cs[:, None]) & (kc < cs[:, None] + WIN_C)
            mask[:, x, j] = np.where(row_ok[:, :, None] & col_ok[:, None, :], 0.0, NEG)
    t = np.arange(GRID)
    row = np.zeros(TP, np.float32)
    col = np.zeros(TP, np.float32)
    row[:GRID] = (t // CB) % ROWS
    col[:GRID] = CB * (t // (CB * ROWS)) + t % CB
    sec = HD // 2
    freqs = (1.0 / (np.float32(10000.0) ** (np.arange(0, sec, 2, dtype=np.float32) / np.float32(sec)))).astype(np.float32)
    d = np.arange(P) % HD
    ang = np.where((d < sec)[:, None], row[None], col[None]) * freqs[d % (sec // 2)][:, None]
    rot = np.zeros((P, P), np.float32)
    for m in range(P):
        if m % sec < sec // 2:
            rot[m + sec // 2, m] = -1.0
        else:
            rot[m - sec // 2, m] = 1.0
    sel = np.zeros((P, 3, P), np.float32)
    for c in range(3):
        for e in range(2 if c < 2 else 1):
            sel[64 * e:64 * e + 64, c, 2 * c + e] = 1.0
    return {
        "ident": np.eye(P, dtype=np.float32),
        "mask": mask.reshape(P, 2, NJ, WR * WC).astype(mybir.dt.np(BF16)),
        "cos": np.cos(ang.astype(np.float32)).astype(np.float32),
        "sin": np.sin(ang.astype(np.float32)).astype(np.float32),
        "rot": rot,
        "sel": sel,
        "bc": np.ascontiguousarray(sel.transpose(2, 1, 0)),
    }


_INS = ["x", "meta_tokens", "norm_mix", "norm_ffn", "norm_final", "a_w_qkv", "a_rel_bias", "a_meta_bias",
        "a_w_o", "b_w_qkv", "b_q_norm", "b_k_norm", "b_w_o", "ffn_w1", "ffn_w3", "ffn_w2"]


def kernel(**inputs):
    import concourse.bacc as bacc
    from concourse.bass_utils import run_bass_kernel_spmd as run

    nc = bacc.Bacc("TRN2", target_bir_lowering=False, num_devices=1)
    arrays, given, consts = {}, {}, {}
    for name in _INS:
        a = np.ascontiguousarray(inputs[name])
        arrays[f"in_{name}"] = a
        given[name] = nc.dram_tensor(f"in_{name}", a.shape, mybir.dt.from_np(a.dtype), kind="ExternalInput").ap()
    for name, a in tables().items():
        arrays[f"table_{name}"] = a
        consts[name] = nc.dram_tensor(f"table_{name}", a.shape, mybir.dt.from_np(a.dtype), kind="ExternalInput").ap()
    out = nc.dram_tensor("out_0", (1, GRID, D), F32, kind="ExternalOutput").ap()
    build(nc, given, consts, out)
    return run(nc, [arrays], core_ids=[0]).results[0]["out_0"]
```

```python
from contextlib import ExitStack

import numpy as np
import concourse.bass as bass
from concourse import mybir
from concourse.alu_op_type import AluOpType as ALU

F32 = mybir.dt.float32
F32R = mybir.dt.float32r
BF16 = mybir.dt.bfloat16
ACT = mybir.ActivationFunctionType
AX = mybir.AxisListType

P = 128
D = 1024
KC = D // P
GRID = 1024
META = 16
T = GRID + META
NB = 3
CW = 348
TP = NB * CW
TW = 9 * P
ROWS, COLS = 16, 64
HR = ROWS // 2
CB = 16
NJ = COLS // CB
WIN_R, WIN_C = 8, 16
WC = 32
K0 = [0, 8, 24, 32]
E0 = [16, 8, 8, 0]
WR = 12
SN = (WR + 1) * WC
KN = (ROWS + 2) * COLS
HD = 64
NH = 16
NPAIR = NH // 2
TILES = 18
FILLS = TILES + 6
HID = 2816
FIT = HID // (2 * P)
EPS = 1e-6
NEG = 1e30
NG = 4
GH = NH // NG
QB = 512
NQB = 9
KT = 9
STEPS = NQB * KT
MT = 33
QW = GH * GRID + P
CLEARS = 2 * (6 + -(-QW // (2 * TP))) + 1
GQ_GROUPS = 10 * NG
V_AT = [4, 5, 6]
H_AT = range(10, 60, 5)
L_AT = [17, 28, 39, 48, 58]
OR = 5
M_AT = [0, 2, 4, 6]
ROW_AT = 8
PB = 4
LAG = 4
ARR, EW = 23, 48


def banks(ap):
    return ap.rearrange("p (b c) -> p b c", b=NB)


def gqa_order():
    order = []
    for g in range(NG + 1):
        new, old = g < NG, g > 0
        order += [("w", g, 0), ("w", g, 1)] if new else []
        order += [("spread", g - 1, 2), ("spread", g - 1, 0), ("rot", g - 1, 2),
                  ("spread", g - 1, 1), ("rot", g - 1, 0)] if old else []
        order += [("w", g, 2)] if new else []
        order += [("rot", g - 1, 1)] if old else []
        order += [("sum", g, 0)] if new else []
    return order


def build(nc, A, C, out):
    es = ExitStack()
    with es:
        def sem(name):
            return es.enter_context(nc.semaphore(name))

        def sb(name, shape, dt, stack=None):
            return (stack or es).enter_context(nc.sbuf_tensor(name, shape, dt))

        h_spill = nc.dram_tensor("h_spill", (P, KC, TP), F32, kind="Internal").ap()
        o_spill = nc.dram_tensor("o_spill", (P, KC, TP), F32, kind="Internal").ap()
        qkv_spill = nc.dram_tensor("qkv_spill", (NG + 1, P, 3, TP), F32, kind="Internal").ap()
        bias_rows = nc.dram_tensor("bias_rows", (NH, CB, ARR, EW), F32, kind="Internal").ap()

        PS = es.enter_context(nc.psum_tensor("PS", [P, 8, 512], F32))
        D0, D1 = 0, 3
        OB = (5, 3)

        uh = sb("uh", [P, KC, TP], F32R)
        ul = sb("ul", [P, KC, TP], F32R)
        wraw = sb("wraw", [P, 2, 512], F32)
        wh = sb("wh", [P, 2, 512], F32R)
        wl = sb("wl", [P, 2, 512], F32R)
        rstd = sb("rstd", [P, TP], F32)
        ssq = sb("ssq", [P, TP], F32)
        ident = sb("ident", [P, P], F32)
        ones = sb("ones", [P, P], F32)
        gains = sb("gains", [P, 5, KC], F32)

        with ExitStack() as st_h:
            h = sb("h", [P, KC, TP], F32, st_h)
            with ExitStack() as st:
                xt = sb("xt", [P, 9, D], F32, st)
                sq_in = sb("sq_in", [P, 2, TP], F32, st)
            with ExitStack() as st:
                at = sb("at", [P, 2, TP], F32, st)
                gh = sb("gh", [P, 2, 2, TP], F32R, st)
                gl = sb("gl", [P, 2, 2, TP], F32R, st)
                sq_ffn = sb("sq_ffn", [P, 2, TP], F32, st)
                fin = sb("fin", [P, 2, D], F32, st)
            with ExitStack() as st:
                oraw = sb("oraw", [P, OR, TP], F32, st)
                oh = sb("oh", [P, KC, TP], F32R, st)
                ol = sb("ol", [P, KC, TP], F32R, st)
                sq_wo = oraw
        with ExitStack() as st:
            keys = sb("keys", [P, KN], F32, st)
            vals = sb("vals", [P, TP], F32, st)
            qs = sb("qs", [P, 2, TW], F32R, st)
            khh = sb("khh", [P, 2, KN], F32R, st)
            kll = sb("kll", [P, 2, KN], F32R, st)
            vt = sb("vt", [P, TILES, P], F32, st)
            vst = sb("vst", [P, TILES, 2, P], F32R, st)
            pth = sb("pth", [P, 2, 4, 2 * P], F32R, st)
            ptl = sb("ptl", [P, 2, 4, 2 * P], F32R, st)
            pmh = sb("pmh", [P, P], F32R, st)
            pml = sb("pml", [P, P], F32R, st)
            pb = sb("pb", [P, 3, 512], F32, st)
            bm = sb("bm", [P, 3, SN], F32, st)
            biasb = sb("biasb", [P, 2, 2, WR * EW], F32, st)
            maskb = sb("maskb", [P, 2, NJ, WR * WC], BF16, st)
            mbn = sb("mbn", [P, NH, 2, WC], F32, st)
            mbp = sb("mbp", [P, 2, 2, WC], F32, st)
            mb_raw = sb("mb_raw", [P, NH * META], F32, st)
            otmp = sb("otmp", [64, 512], F32, st)
            ob = sb("ob", [P, TP], F32, st)
            small = sb("small", [P, 3, 4], F32, st)
        with ExitStack() as st:
            cosb = sb("cosb", [P, TP], F32, st)
            sinb = sb("sinb", [P, TP], F32, st)
            selb = sb("selb", [P, 3, P], F32, st)
            bcb = sb("bcb", [P, 3, P], F32, st)
            rotb = sb("rotb", [P, P], F32, st)
            gnb = sb("gnb", [P, 2], F32, st)
            tq = sb("tq", [P, 2, 3, TP], F32, st)
            tn = sb("tn", [P, 2, 3, TP], F32, st)
            nwt = sb("nwt", [P, 2, TP], F32, st)
        with ExitStack() as st:
            ones_r = sb("ones_r", [P, P], F32R, st)
            tqb = sb("tqb", [P, 2, TP], F32, st)
            tkv = sb("tkv", [P, TW], F32, st)
            uhf = uh[:, :, :].rearrange("p k t -> p (k t)")
            ulf = ul[:, :, :].rearrange("p k t -> p (k t)")
            qh = [sb("qh0", [P, QW], F32R, st)[:, :], uhf[:, 0:QW]]
            qx = [sb("qx0", [P, QW], F32R, st)[:, :], ulf[:, 0:QW]]
            ks = [sb("ks0", [P, TW], F32R, st)[:, :], uhf[:, QW:QW + TW]]
            kx = [sb("kx0", [P, TW], F32R, st)[:, :], uhf[:, QW + TW:QW + 2 * TW]]
            vg = [sb("vg0", [P, KT, P], F32R, st)[:, :, :],
                  ulf[:, QW:QW + KT * P].rearrange("p (t d) -> p t d", d=P)]
            pf = sb("pf", [P, PB, QB], F32, st)
            ph = sb("ph", [P, PB, QB], F32R, st)
            pl = sb("pl", [P, PB, QB], F32R, st)
            acc = sb("acc", [P, 2, QB], F32, st)
            nmx = sb("nmx", [P, 4], F32, st)
            dgm = sb("dgm", [P, 4, P], F32R, st)
            rsm = sb("rsm", [P, 4], F32, st)
            dgs = sb("dgs", [P, 4, P], F32, st)
            ot1 = sb("ot1", [64, QB], F32, st)
            ob2 = sb("ob2", [P, 2, TP], F32, st)

        s_id = sem("ident_loaded")
        s_const = sem("gains_loaded")
        s_raw = [sem("raw_slot0_loaded"), sem("raw_slot1_loaded")]
        s_rawk = [sem("raw_slot0_k_loaded"), sem("raw_slot1_k_loaded")]
        s_whi = sem("weight_hi_made")
        s_wrd = sem("weight_ready")
        s_un = sem("unit_multiplied")
        s_df = sem("group_read")
        s_dv = sem("sum_inverted")
        s_car = sem("tile_waits_over")
        s_sq = sem("square_made")
        s_uh = sem("u_hi_made")
        s_ur = sem("u_ready")
        s_acc = sem("squares_added")
        s_ssq = sem("squares_summed")
        s_st = sem("stat_done")
        s_rt = sem("root_taken")
        s_rs = sem("rstd_ready")
        s_nw = sem("refinement_step")
        s_qsp = [sem(f"qkv_chunk{c}_spilled") for c in range(3)]
        s_qld = sem("qkv_loaded")
        s_vgl = sem("gqa_v_ready")
        s_vt = sem("gqa_v_transposed")
        s_xl = [sem(f"x_tile{i}_loaded") for i in range(9)]
        s_xt = sem("x_transposed")
        s_xra = sem("x_bank6_read")
        s_xrb = sem("x_bank7_read")
        s_pad = sem("pad_zeroed")
        s_silu = sem("silu_made")
        s_gh = sem("g_hi_made")
        s_gr = sem("g_ready")
        s_hsp = sem("h_spilled")
        s_hld = sem("h_loaded")
        s_osp = sem("o_spilled")
        s_old = [sem(f"o_buffer{i}_loaded") for i in range(OR)]
        s_oh = sem("o_hi_made")
        s_or = sem("o_ready")
        s_fs = sem("final_scaled")
        s_ft = sem("final_transposed")
        s_fca = sem("final_bank6_copied")
        s_fcb = sem("final_bank7_copied")
        s_out = [sem(f"out_stored_from_buffer{i}") for i in range(2)]

        U_NA, U_WO, U_FF, U_GQ = 0, [48, 264], [64, 280], 240
        G_NA, G_GQ = 1, 167
        G_WO, G_FF = [25, G_GQ + GQ_GROUPS], [34, G_GQ + GQ_GROUPS + 9]
        G_ST = [0, 33, 166, G_FF[1] - 1, G_FF[1] + 132]

        def kview(ap):
            return ap.rearrange("(k p) c -> p k c", p=P)

        w_qkv, w_qkv_b = kview(A["a_w_qkv"][0]), kview(A["b_w_qkv"][0])
        w_kv = w_qkv_b[:, :, NH * HD:].rearrange("p k (s c) -> p k s c", s=2)
        w_o = [kview(A["a_w_o"][0]), kview(A["b_w_o"][0])]
        w_1 = [kview(A["ffn_w1"][l]) for l in range(2)]
        w_3 = [kview(A["ffn_w3"][l]) for l in range(2)]
        w_2 = [kview(A["ffn_w2"][l]) for l in range(2)]
        x_g = A["x"][0].rearrange("(s r c) d -> s r c d", s=2, c=COLS)
        out_g = out[0].rearrange("(s r c) d -> s r c d", s=2, c=COLS)

        order = gqa_order()

        s_zero = sem("attention_memory_cleared")
        s_bfill = sem("bias_rows_filled")
        s_brow = sem("bias_rows_written")
        s_bload = [sem("bias_of_head0_loaded"), sem("bias_of_head1_loaded")]
        s_na = sem("na_consts_loaded")
        s_mbn = sem("meta_bias_made")
        s_qhi = sem("q_hi_made")
        s_qlo = sem("q_lo_made")
        s_kn = sem("k_in_grid_order")
        s_khi = sem("k_hi_made")
        s_klo = sem("k_lo_made")
        s_klc = sem("k_lo_copied")
        s_vs = sem("v_strips_made")
        s_mbp = sem("pair_meta_bias_made")
        s_bm = sem("tile_bias_made")
        s_s = sem("scores_done")
        s_sb = sem("scores_biased")
        s_ex = sem("exp_done")
        s_pr = sem("p_ready")
        s_tf = sem("bank_transposed")
        s_th = sem("t_hi_made")
        s_tl = sem("t_lo_made")
        s_pv = sem("pv_done")
        s_oa = sem("o_lo_part_copied")
        s_ob = sem("o_made")
        s_gc = sem("gqa_consts_loaded")
        s_gmem = sem("gqa_float_memory_cleared")
        s_gz = sem("gqa_operands_cleared")
        s_gsq = sem("qk_squared")
        s_gsr = sem("qk_root_taken")
        s_grc = sem("qk_rstd_ready")
        s_ga = sem("aux_product_done")
        s_vgh = sem("gqa_v_hi_made")
        s_rot = sem("qk_rotated")
        s_gqh = sem("gqa_hi_made")
        s_gql = sem("gqa_lo_made")
        s_mx = sem("max_scores_done")
        s_mr = sem("max_taken")
        s_dg = sem("max_diagonal_made")
        s_mrow = sem("max_row_spread")
        s_mset = sem("max_row_set")
        s_sc = sem("gqa_scores_done")
        s_gex = sem("gqa_exp_done")
        s_gph = sem("gqa_p_hi_made")
        s_gpl = sem("gqa_p_ready")
        s_gacc = sem("gqa_p_added")
        s_gpv = sem("gqa_pv_done")
        s_gsum = sem("gqa_sums_done")
        s_gdr = sem("sum_diagonal_made")
        s_gspr = sem("sum_row_spread")
        s_goa = sem("gqa_o_lo_part_copied")
        s_gob = sem("gqa_o_made")
        s_gc2 = sem("k_gain_loaded")
        s_gs1 = sem("gqa_hi_parts")
        s_gs2 = sem("gqa_small_parts")
        s_cs = sem("cosine_part_made")
        s_gnb = sem("q_gain_scaled")
        s_rsm = sem("sums_inverted")
        s_gds = sem("sum_diagonal_parts")
        s_got = sem("o_halves_added")
        s_sr = sem("silu_scaled")

        block = es.enter_context(nc.Block())

        @block.sync
        def _(sp):
            def fetch(n, slot, src):
                if not (isinstance(n, int) and n < 2):
                    sp.wait_ge(s_wrd, n - 1)
                if len(src.shape) == 4:
                    dst = wraw[:, slot, :].rearrange("p (k s c) -> p k s c", s=2, c=HD)
                    sp.dma_start(dst[:, :, 0, :], src[:, :, 0, :]).then_inc(s_rawk[slot], 16)
                    sp.dma_start(dst[:, :, 1, :], src[:, :, 1, :]).then_inc(s_raw[slot], 16)
                    return
                dst = wraw[:, slot, 0:src.shape[1] * P].rearrange("p (k c) -> p k c", c=P)
                sp.dma_start(dst, src).then_inc(s_raw[slot], 16)

            def fetch_chunk(n, w, c0):
                for j in range(2):
                    fetch(n + j, j, w[:, 4 * j:4 * j + 4, bass.ds(c0, P)])

            def fetch_up(n, l, it):
                for b in range(2):
                    fetch_chunk(n + 4 * b, w_1[l], 2 * P * it + P * b)
                    fetch_chunk(n + 4 * b + 2, w_3[l], 2 * P * it + P * b)

            def fetch_down(n, l, it):
                for m in range(KC):
                    fetch(n + m, m % 2, w_2[l][:, bass.ds(2 * it, 2), P * m:P * m + P])

            def fetch_ffn(l):
                fetch_up(U_FF[l], l, 0)
                with sp.Fori(0, FIT - 1) as i:
                    fetch_up(16 * i + (U_FF[l] + 8), l, i + 1)
                    fetch_down(16 * i + (U_FF[l] + 16), l, i)
                fetch_down(U_FF[l] + 168, l, FIT - 1)

            def fetch_wo(l, m0=0):
                with sp.Fori(m0, KC) as m:
                    fetch_chunk(2 * m + U_WO[l], w_o[l], P * m)

            def load_bias(p, hd):
                for x in range(2):
                    for r in range(HR):
                        a0 = (7 if x else 11) - r
                        sp.dma_start(
                            biasb[CB * r:CB * r + CB, hd, x, :].rearrange("p (a e) -> p a e", e=EW),
                            bias_rows[bass.ds(2 * p + hd, 1), :, a0:a0 + WR, :]
                            .rearrange("h c a e -> (h c) a e")).then_inc(s_bload[hd], 16)

            sp.dma_start(ident[:, :], C["ident"]).then_inc(s_id, 16)
            for i in range(8):
                sp.dma_start(xt[:, i, :],
                             x_g[i % 2, :, CB * (i // 2):CB * (i // 2) + CB, :]).then_inc(s_xl[i], 16)
            sp.dma_start(xt[0:META, 8, :], A["meta_tokens"]).then_inc(s_xl[8], 16)
            fetch_chunk(0, w_qkv, 2 * D)
            sp.wait_ge(s_pad, 2)
            sp.wait_ge(s_xra, 9)
            sp.wait_ge(s_xrb, 9)
            for m in range(KC):
                sp.dma_start(h_spill[:, m, :], h[:, m, :]).then_inc(s_hsp, 16)
            fetch_chunk(2, w_qkv, D)
            fetch_chunk(4, w_qkv, 0)
            sp.wait_ge(s_brow, 16 * CB)
            load_bias(0, 0)
            load_bias(0, 1)
            with sp.Fori(0, NPAIR - 1) as p:
                fetch_chunk(6 * p + 6, w_qkv, P * p + (P + 2 * D))
                fetch_chunk(6 * p + 8, w_qkv, P * p + (P + D))
                sp.wait_ge(s_bm, 34 * p + 17)
                load_bias(p + 1, 0)
                fetch_chunk(6 * p + 10, w_qkv, P * p + P)
                sp.wait_ge(s_bm, 34 * p + 34)
                load_bias(p + 1, 1)
            fetch_wo(0)
            fetch_ffn(0)
            with sp.Fori(0, NG) as g:
                for c in range(2):
                    fetch_chunk(6 * g + (U_GQ + 2 * c), w_qkv_b, 2 * P * g + P * c)
                for j in range(2):
                    fetch(6 * g + (U_GQ + 4 + j), j, w_kv[:, 4 * j:4 * j + 4, :, bass.ds(HD * g, HD)])
            for m in range(2):
                fetch_chunk(U_WO[1] + 2 * m, w_o[1], P * m)
            with sp.Fori(0, NG) as g:
                sp.wait_ge(s_gob, NQB * g + NQB)
                sp.dma_start(o_spill[:, bass.ds(2 * g, 2), :], ob2[:, :, :]).then_inc(s_osp, 16)
            fetch_wo(1, 2)
            fetch_ffn(1)
            for i in range(8):
                sp.wait_ge(s_fca, i + 1)
                sp.wait_ge(s_fcb, i + 1)
                sp.dma_start(out_g[i % 2, :, CB * (i // 2):CB * (i // 2) + CB, :],
                             fin[:, i % 2, :]).then_inc(s_out[i % 2], 16)
            for stored in s_out:
                sp.wait_ge(stored, 16 * 4)

        @block.gpsimd
        def _(po):
            def split(n, slot, loads, w=512):
                po.wait_ge(s_raw[slot], 16 * loads)
                if not (isinstance(n, int) and n < 2):
                    po.wait_ge(s_un, n - 1)
                nc.gpsimd.tensor_tensor(wh[:, slot, 0:w], wraw[:, slot, 0:w],
                                        ones[:, 0:1].to_broadcast([P, w]), ALU.mult).then_inc(s_whi, 1)
                po.wait_ge(s_whi, n + 1)
                nc.gpsimd.tensor_tensor(wl[:, slot, 0:w], wraw[:, slot, 0:w],
                                        wh[:, slot, 0:w].bitcast(F32), ALU.subtract).then_inc(s_wrd, 1)

            def split_pair(n, half, w=512, kv=None):
                if kv is not None:
                    for k_loaded in s_rawk:
                        po.wait_ge(k_loaded, 16 * (kv + 1))
                split(n, 0, half + 1, w)
                split(n + 1, 1, half + 1, w)

            def split_ffn(l):
                n0 = U_FF[l]
                with po.Fori(0, 4) as i:
                    split_pair(2 * i + n0, i + n0 // 2)
                with po.Fori(0, FIT - 1) as i:
                    for q in range(4):
                        split_pair(16 * i + (n0 + 8 + 2 * q), 8 * i + (n0 // 2 + 4 + q))
                    for q in range(4):
                        split_pair(16 * i + (n0 + 16 + 2 * q), 8 * i + (n0 // 2 + 8 + q), 2 * P)
                with po.Fori(0, 4) as i:
                    split_pair(2 * i + (n0 + 168), i + (n0 // 2 + 84), 2 * P)

            def split_wo(l):
                with po.Fori(1, KC) as i:
                    split_pair(2 * i + U_WO[l], i + U_WO[l] // 2)

            po.wait_ge(s_pad, 2)
            split_pair(0, 0)
            split_pair(2, 1)
            po.wait_ge(s_hsp, 16 * KC)
            po.wait_ge(s_ur, KC)
            for t in (keys[:, :], vt[:, :, :], pb[:, :, :], ob[:, :]):
                nc.gpsimd.memset(t, 0.0).then_inc(s_zero, 1)
            nc.gpsimd.memset(mbn[:, :, :, :], NEG).then_inc(s_zero, 1)
            po.wait_ge(s_zero, 5)
            nc.gpsimd.tensor_copy(qs[:, :, TP:TW], vt[:, 0:2, 0:TW - TP]).then_inc(s_zero, 1)
            po.wait_ge(s_zero, 6)
            po.wait_ge(s_bfill, 16)

            def strips():
                for j in range(NJ):
                    dst = vt[:, 4 * j:4 * j + 4, :].rearrange("p a (b c) -> p (a b) c", c=WC)
                    for b in range(NJ):
                        lo, hi = max(K0[j], CB * b), min(K0[j] + WC, CB * b + CB)
                        if lo < hi:
                            src = vals[:, 256 * b:256 * b + 256].rearrange("p (r c) -> p r c", c=CB)
                            yield dst[:, :, lo - K0[j]:hi - K0[j]], src[:, :, lo - CB * b:hi - CB * b]

            def pair_meta_bias(p):
                nc.gpsimd.tensor_copy(mbp[:, :, :, :], mbn[:, bass.ds(2 * p, 2), :, :]).then_inc(s_mbp, 1)

            def make_strips(p, part, parts):
                jobs = list(strips())
                if part == 0:
                    po.wait_ge(s_df, 3 * p + (G_NA + 1))
                    po.wait_ge(s_tf, FILLS * (p - 1) + 6 if not isinstance(p, int) else 0)
                    for cls, at_ in ((0, 8), (1, 0)):
                        nc.gpsimd.tensor_tensor(vt[:, 16 + cls, at_:at_ + META], vals[:, GRID:T],
                                                ones[:, 0:META], ALU.mult).then_inc(s_vs, 1)
                for dst, src in jobs[part::parts]:
                    nc.gpsimd.tensor_copy(dst, src).then_inc(s_vs, 1)

            def tile_bias(p, u):
                hd, v = u // 9, u % 9
                if v == 0:
                    po.wait_ge(s_bload[hd], 32 * HR * (p + 1))
                po.wait_ge(s_mbp, p + 1)
                po.wait_ge(s_sb, TILES * p + max(u - 2, 0))
                j, x = v // 2, v % 2
                if v == 8:
                    nc.gpsimd.tensor_tensor(bm[:, u % 3, 0:WC], mbp[:, hd, 0, :], ones[:, 0:WC],
                                            ALU.mult).then_inc(s_bm, 1)
                    return
                o, m_at = (0, WR * WC) if x else (WC, 0)
                nc.gpsimd.tensor_tensor(
                    bm[:, u % 3, o:o + WR * WC].rearrange("p (r c) -> p r c", c=WC),
                    maskb[:, x, j, :].rearrange("p (r c) -> p r c", c=WC),
                    biasb[:, hd, x, :].rearrange("p (r c) -> p r c", c=EW)[:, :, E0[j]:E0[j] + WC],
                    ALU.subtract).then_inc(s_bm, 1)
                nc.gpsimd.tensor_copy(bm[:, u % 3, m_at:m_at + WC], mbp[:, hd, j % 2, :]).then_inc(s_bm, 1)

            def attend_pair(p, more):
                for u in range(TILES):
                    if more:
                        if u == 2:
                            split_pair(6 * p + 6, 3 * p + 3)
                        for at_, n in ((7, 8), (11, 9), (16, 10)):
                            if u == at_:
                                split(6 * p + n, n % 2, 3 * p + (n // 2 + 1))
                        if u >= 12:
                            make_strips(p + 1, u - 12, 6)
                    elif u == 6:
                        split_pair(U_WO[0], U_WO[0] // 2)
                    tile_bias(p, u)
                if more:
                    po.wait_ge(s_bm, 34 * p + 34)
                    split(6 * p + 11, 1, 3 * p + 6)
                    pair_meta_bias(p + 1)

            po.wait_ge(s_mbn, 2)
            pair_meta_bias(0)
            make_strips(0, 0, 1)
            split_pair(4, 2)
            with po.Fori(0, NPAIR - 1) as p:
                attend_pair(p, True)
            attend_pair(NPAIR - 1, False)
            split_wo(0)
            split_ffn(0)
            split_pair(U_GQ, U_GQ // 2)
            with po.Fori(0, NG - 1) as g:
                split_pair(6 * g + (U_GQ + 2), 3 * g + (U_GQ // 2 + 1))
                split_pair(6 * g + (U_GQ + 4), 3 * g + (U_GQ // 2 + 2), kv=g)
                split_pair(6 * g + (U_GQ + 6), 3 * g + (U_GQ // 2 + 3))
            split_pair(6 * NG + (U_GQ - 4), 3 * NG + (U_GQ // 2 - 2))
            split_pair(6 * NG + (U_GQ - 2), 3 * NG + (U_GQ // 2 - 1), kv=NG - 1)
            split_pair(U_WO[1], U_WO[1] // 2)
            for spilled in s_qsp:
                po.wait_ge(spilled, 16 * NG + 16)
            for t in (tkv[:, :], ob2[:, :, :]):
                nc.gpsimd.memset(t, 0.0).then_inc(s_gmem, 1)
            def attend(g):
                for s in range(STEPS):
                    b, kt = divmod(s, KT)
                    n = QB if b < 8 else P
                    if kt == 0:
                        continue
                    po.wait_ge(s_gex, STEPS * g + (s + 1))
                    cur = pf[:, s % PB, 0:n]
                    if kt == 1:
                        po.wait_ge(s_gsum, NQB * g + max(b - 1, 0))
                        ins = nc.gpsimd.tensor_tensor(acc[:, b % 2, 0:n], pf[:, (s - 1) % PB, 0:n], cur, ALU.add)
                    else:
                        po.wait_ge(s_gacc, 8 * NQB * g + (8 * b + kt - 1))
                        q = slice(0, META) if kt == KT - 1 else slice(0, P)
                        ins = nc.gpsimd.tensor_tensor(acc[q, b % 2, 0:n], acc[q, b % 2, 0:n],
                                                      pf[q, s % PB, 0:n], ALU.add)
                    ins.then_inc(s_gacc, 1)
            with po.Fori(0, NG) as g:
                attend(g)
            split_wo(1)
            split_ffn(1)

        @block.tensor
        def _(pe):
            def unit(n, slot, set_, xh, xl, ks_, first, last):
                pe.wait_ge(s_wrd, n + 1)
                for i, k in enumerate(ks_):
                    a, b = wh[:, slot, P * i:P * i + P], wl[:, slot, P * i:P * i + P]
                    for ti, (w, x) in enumerate(((a, xh), (a, xl), (b, xh))):
                        for c in range(NB):
                            mm = nc.tensor.matmul(
                                PS[:, set_ + c, 0:CW], w, x[k][:, c * CW:(c + 1) * CW],
                                start=(first and i == 0 and ti == 0),
                                stop=(last and i == len(ks_) - 1 and ti == 2))
                mm.then_inc(s_un, 1)

            def dense(n, set_, xh, xl, need):
                pe.wait_ge(s_df, need)
                for j in range(2):
                    unit(n + j, j, set_, xh, xl, range(4 * j, 4 * j + 4), j == 0, j == 1)

            uhc, ulc = [uh[:, k, :] for k in range(KC)], [ul[:, k, :] for k in range(KC)]

            def spread(set_, w, x):
                for c in range(NB):
                    mm = nc.tensor.matmul(PS[:, set_ + c, 0:CW], w, x[:, c * CW:(c + 1) * CW],
                                          start=True, stop=True)
                return mm

            def stat(k):
                pe.wait_ge(s_ssq, k + 1)
                if k:
                    pe.wait_ge(s_df, G_ST[k])
                spread(D1, ones[:, :], ssq[:, :]).then_inc(s_st, 1)

            def ffn(l):
                ub, gb = U_FF[l], G_FF[l]

                def up(n, g, first=0):
                    for b in range(2):
                        for q, set_ in ((0, D0), (1, D1)):
                            dense(n + 4 * b + 2 * q, set_, uhc, ulc, g + (2 * b + q - 1 + (first and not b and not q)))

                def down(n, g, k, par):
                    pe.wait_ge(s_gr, k)
                    xh, xl = [gh[:, par, b, :] for b in range(2)], [gl[:, par, b, :] for b in range(2)]
                    for m in range(KC):
                        pe.wait_ge(s_df, g + (m - 1))
                        unit(n + m, m % 2, D1 if m % 2 else D0, xh, xl, range(2), True, True)

                pe.wait_ge(s_ur, KC * (2 * l + 2))
                up(ub, gb, 1)
                with pe.Fori(0, FIT // 2) as i:
                    for s in range(2):
                        up(32 * i + (ub + 8 + 16 * s), 24 * i + (gb + 4 + 12 * s))
                        down(32 * i + (ub + 16 + 16 * s), 24 * i + (gb + 8 + 12 * s),
                             4 * i + (2 * FIT * l + 2 * s + 2), s)
                down(ub + 168, gb + 124, 2 * FIT * (l + 1), 0)

            def proj_out(l):
                ohc, olc = [oh[:, k, :] for k in range(KC)], [ol[:, k, :] for k in range(KC)]
                pe.wait_ge(s_df, G_WO[l])
                with pe.Fori(0, KC // 2) as i:
                    for b, set_ in ((0, D0), (1, D1)):
                        n = 4 * i + (U_WO[l] + 2 * b)
                        pe.wait_ge(s_df, 2 * i + (G_WO[l] + b - 1))
                        for j in range(2):
                            pe.wait_ge(s_or, KC * l + 4 * (j + 1))
                            unit(n + j, j, set_, ohc, olc, range(4 * j, 4 * j + 4), j == 0, j == 1)

            pe.wait_ge(s_id, 16)
            for i in range(9):
                n = P if i < 8 else META
                pe.wait_ge(s_xl[i], 16)
                for f in range(2):
                    if i:
                        pe.wait_ge(s_xrb if f else s_xra, i)
                    for c in range(4):
                        k = 4 * f + c
                        mm = nc.tensor.transpose(PS[:, 6 + f, c * n:(c + 1) * n],
                                                 xt[0:n, i, k * P:(k + 1) * P], ident[0:n, 0:n])
                    mm.then_inc(s_xt, 1)
            pe.wait_ge(s_pad, 2)
            stat(0)

            k3 = [khh[:, hd, :].rearrange("p (r c) -> p r c", c=COLS) for hd in range(2)]
            l3 = [kll[:, hd, :].rearrange("p (r c) -> p r c", c=COLS) for hd in range(2)]
            def filler(n, c, need):
                slot, i = divmod(c, 4)
                if c == 0:
                    pe.wait_ge(s_df, need)
                if i == 0:
                    pe.wait_ge(s_wrd, n + slot + 1)
                a, b = wh[:, slot, P * i:P * i + P], wl[:, slot, P * i:P * i + P]
                for ti, (w, x) in enumerate(((a, uhc), (a, ulc), (b, uhc))):
                    for bk in range(NB):
                        mm = nc.tensor.matmul(PS[:, D0 + bk, 0:CW], w, x[c][:, bk * CW:(bk + 1) * CW],
                                              start=(c == 0 and ti == 0), stop=(c == 7 and ti == 2),
                                              skip_group_check=True)
                if i == 3:
                    mm.then_inc(s_un, 1)

            def attend_pair(p, more):
                g = 3 * p + G_NA
                dense(6 * p + 4, D0, uhc, ulc, g + 2)

                def scores(u):
                    hd, v = u // 9, u % 9
                    pe.wait_ge(s_sb, TILES * p + max(u - 1, 0))
                    for i, k in enumerate((k3[hd], l3[hd])):
                        if v < 8:
                            j, x = v // 2, v % 2
                            mm = nc.tensor.matmul(PS[:, 6 + u % 2, 0:SN], qs[:, hd, P * v:P * v + P],
                                                  k[:, 5 * x:5 * x + WR + 1, K0[j]:K0[j] + WC],
                                                  start=(i == 0), stop=(i == 1))
                        else:
                            mm = nc.tensor.matmul(PS[:, 6 + u % 2, 0:WC], qs[:, hd, GRID:GRID + P],
                                                  k[:, 0, 0:WC], start=(i == 0), stop=(i == 1))
                    mm.then_inc(s_s, 1)

                def fill(f, tiles):
                    pe.wait_ge(s_tl, FILLS * p + max(f - 1, 0))
                    for c, t in enumerate(tiles):
                        mm = nc.tensor.transpose(PS[:, 3 + f % 2, P * c:P * c + P], t, ident[:, :])
                    mm.then_inc(s_tf, 1)

                def probs(u):
                    v = u % 9
                    pe.wait_ge(s_pr, TILES * p + (u + 1))
                    if v == 8:
                        at_ = [0]
                    elif v % 2:
                        at_ = [384, 0, 128, 256]
                    else:
                        at_ = [WC, WC + 128, WC + 256, 0]
                    fill(6 + u, [pb[:, u % 3, a:a + P] for a in at_])

                def pv(i):
                    hd, v = i // 5, i % 5
                    last_u = 9 * hd + (2 * v + 1 if v < 4 else 8)
                    pe.wait_ge(s_tl, FILLS * p + (7 + last_u))
                    if v in (0, 2, 4):
                        pe.wait_ge(s_ob, 6 * p + (3 * hd + v // 2))
                    if v == 4:
                        for i2, t in enumerate((pmh, pml)):
                            mm = nc.tensor.matmul(PS[:, 5, 0:P], vst[:, 16, hd, :], t[:, :],
                                                  start=(i2 == 0), stop=(i2 == 1))
                        mm.then_inc(s_pv, 1)
                        return
                    o0 = 256 * (v % 2)
                    sl = (4 * hd + v) % 2
                    for i2, t in enumerate((pth, ptl)):
                        parts = [(4 * v + 1, 1, 0, 256), (4 * v + 2, 2, 0, 256), (4 * v, 0, 0, 128),
                                 (4 * v + 3, 3, 128, 256), (16 + v % 2, 3, 0, 128), (16 + v % 2, 0, 128, 256)]
                        for i3, (tile, idx, a, b) in enumerate(parts):
                            mm = nc.tensor.matmul(PS[:, 5, o0 + a:o0 + b], vst[:, tile, hd, :],
                                                  t[:, sl, idx, a:b], start=(i2 == 0 and i3 == 0),
                                                  stop=(i2 == 1 and i3 == 5), skip_group_check=True)
                    mm.then_inc(s_pv, 1)

                pe.wait_ge(s_vs, 12 * p + 12)
                fills = [[vt[:, 3 * f + c, :] for c in range(3)] for f in range(6)]
                fill(0, fills[0])
                fill(1, fills[1])
                pe.wait_ge(s_qlo, 2 * p + 2)
                pe.wait_ge(s_klc, 2 * p + 2)
                scores(0)
                scores(1)
                for f in range(2, 6):
                    fill(f, fills[f])
                due = {9 * hd + (2 * v + 1 if v < 4 else 8) + 1: 5 * hd + v for hd in range(2) for v in range(5)}
                for u in range(TILES):
                    probs(u)
                    if u + 2 < TILES:
                        scores(u + 2)
                    if u in due:
                        pv(due[u])
                    if more and u < 8:
                        filler(6 * p + 6, u, g + 3)
                    elif more and 9 <= u < 17:
                        filler(6 * p + 8, u - 9, g + 4)
                pv(9)

            dense(0, D0, uhc, ulc, G_NA)
            dense(2, D0, uhc, ulc, G_NA + 1)
            with pe.Fori(0, NPAIR - 1) as p:
                attend_pair(p, True)
            attend_pair(NPAIR - 1, False)
            proj_out(0)
            stat(1)
            ffn(0)
            stat(2)

            pe.wait_ge(s_gc, 16 * 7)
            for n, (what, g, c) in enumerate(order):
                set_ = D1 if n % 2 else D0
                if what == "w":
                    dense(6 * g + U_GQ + 2 * c, set_, uhc, ulc, G_GQ + n - 1)
                    continue
                pe.wait_ge(s_df, G_GQ + n - 1)
                x = tn[:, g % 2, c, :]
                if what == "sum":
                    pe.wait_ge(s_gsq, 3 * g + 3)
                    for i in range(3):
                        for b in range(NB):
                            mm = nc.tensor.matmul(PS[:, set_ + b, 0:CW], selb[:, i, :],
                                                  tn[:, g % 2, i, b * CW:(b + 1) * CW],
                                                  start=(i == 0), stop=(i == 2))
                    mm.then_inc(s_ga, 1)
                elif what == "spread":
                    pe.wait_ge(s_grc, g + 1)
                    spread(set_, bcb[:, c, :], ssq[:, :]).then_inc(s_ga, 1)
                else:
                    pe.wait_ge(s_df, G_GQ + order.index(("spread", g, c)) + 1)
                    spread(set_, rotb[:, :], x).then_inc(s_ga, 1)

            pe.wait_ge(s_gz, CLEARS)
            def tile_max(g, par, b, i):
                t = 4 * b + i
                pe.wait_ge(s_mr, MT * g + t)
                for c, k0 in enumerate((0, CW, T - CW)):
                    mm = nc.tensor.matmul(PS[:, c, 0:CW], qh[par][:, P * t:P * t + P],
                                          ks[par][:, k0:k0 + CW], start=True, stop=True)
                mm.then_inc(s_mx, 1)

            def max_row(g, b):
                nt = 4 if b < 8 else 1
                pe.wait_ge(s_dg, MT * g + (4 * b + nt))
                for i in range(nt):
                    mm = nc.tensor.matmul(PS[:, 4, P * i:P * i + P], ones_r[:, :], dgm[:, i, :],
                                          start=True, stop=True)
                mm.then_inc(s_mrow, 1)

            def v_by_key(g, f):
                pe.wait_ge(s_qld, 48 * g + 48)
                if f or not isinstance(g, int):
                    pe.wait_ge(s_vgl, 3 * g + f)
                for i, t in enumerate(range(4 * f, min(4 * f + 4, KT))):
                    mm = nc.tensor.transpose(PS[:, 4, P * i:P * i + P], tkv[:, P * t:P * t + P], ident[:, :])
                mm.then_inc(s_vt, 1)

            def attend(g, par):
                def cols(b):
                    return slice(QB * b, QB * b + (QB if b < 8 else P))

                def sums(b):
                    nt = 4 if b < 8 else 1
                    pe.wait_ge(s_gacc, 8 * NQB * g + 8 * (b + 1))
                    pe.wait_ge(s_mset, NQB * g + (b + 2))
                    if b + 1 in V_AT:
                        pe.wait_ge(s_vgl, 3 * g + (4 + V_AT.index(b + 1)))
                    for i in range(nt):
                        mm = nc.tensor.matmul(PS[:, 4, i:i + 1], acc[:, b % 2, P * i:P * i + P], ones[:, 0:1],
                                              start=True, stop=True)
                    mm.then_inc(s_gsum, 1)

                def sums_row(b):
                    nt = 4 if b < 8 else 1
                    pe.wait_ge(s_gdr, NQB * g + (b + 1))
                    for i in range(nt):
                        mm = nc.tensor.matmul(PS[:, 4, P * i:P * i + P], ones[:, :], dgs[:, i, :],
                                              start=True, stop=True)
                    mm.then_inc(s_gspr, 1)

                pe.wait_ge(s_vgl, 3 * g + 3)
                for s in range(STEPS + LAG):
                    b, kt = divmod(s, KT)
                    if s < STEPS:
                        pe.wait_ge(s_gex, STEPS * g + max(s - 1, 0))
                        n = QB if b < 8 else P
                        for i, (k, q) in enumerate(((ks[par], qh[par]), (kx[par], qx[par]))):
                            if kt == 0 and i:
                                pe.wait_ge(s_mset, NQB * g + (b + 1))
                            mm = nc.tensor.matmul(PS[:, 6 + s % 2, 0:n], k[:, P * kt:P * kt + P], q[:, cols(b)],
                                                  start=(i == 0), stop=(i == 1))
                        mm.then_inc(s_sc, 1)
                        if kt == 0 and b in V_AT:
                            v_by_key(g + 1, V_AT.index(b))
                        nb = (g, par, b + 1) if b < 8 else (g + 1, 1 - par, 0)
                        if kt == 0 and b == 8:
                            pe.wait_ge(s_gql, 5 * g + 10)
                            pe.wait_ge(s_gqh, 5 * g + 10)
                        if kt in M_AT and not (b == 7 and kt):
                            tile_max(*nb, M_AT.index(kt))
                        if kt == ROW_AT:
                            pe.wait_ge(s_gob, NQB * g + b)
                            max_row(nb[0], nb[2])
                    if s >= LAG:
                        b2, kt2 = divmod(s - LAG, KT)
                        n = QB if b2 < 8 else P
                        pe.wait_ge(s_gpl, STEPS * g + (s - LAG + 1))
                        if kt2 == 0:
                            pe.wait_ge(s_gob, NQB * g + max(b2 - 1, 0))
                        for i, t in enumerate((ph, pl)):
                            mm = nc.tensor.matmul(PS[:, OB[b2 % 2], 0:n], vg[par][:, kt2, :], t[:, (s - LAG) % PB, 0:n],
                                                  start=(kt2 == 0 and i == 0), stop=(kt2 == 8 and i == 1))
                        mm.then_inc(s_gpv, 1)
                        if kt2 == 8:
                            sums(b2)
                        if b2 and kt2 == 0:
                            sums_row(b2 - 1)
                sums_row(NQB - 1)
            for f in range(3):
                v_by_key(0, f)
            pe.wait_ge(s_gql, 5)
            pe.wait_ge(s_gqh, 5)
            for i in range(4):
                tile_max(0, 0, 0, i)
            pe.wait_ge(s_vgl, 3)
            max_row(0, 0)
            with pe.Fori(0, NG // 2) as i:
                for par in range(2):
                    attend(2 * i + par, par)
            proj_out(1)
            stat(3)
            ffn(1)
            stat(4)
            for i in range(8):
                pe.wait_ge(s_fs, KC * (i // 4 + 1))
                for f in range(2):
                    if i:
                        pe.wait_ge(s_fcb if f else s_fca, i)
                    for c in range(4):
                        mm = nc.tensor.transpose(PS[:, 6 + f, P * c:P * c + P],
                                                 h[:, 4 * f + c, P * i:P * i + P], ident[:, :])
                    mm.then_inc(s_ft, 1)

        @block.scalar
        def _(act):
            def squares(k, m, buf, sem_, need):
                act.wait_ge(sem_, need)
                if m >= 2:
                    act.wait_ge(s_acc, (KC - 1) * k + m - 1)
                nc.scalar.activation(buf[:, m % 2, :], h[:, m, :], ACT.Square).then_inc(s_sq, 1)
                if k < 4:
                    nc.scalar.activation(uh[:, m, :], h[:, m, :], ACT.Copy,
                                         scale=gains[:, k, m:m + 1]).then_inc(s_uh, 1)

            def root(k):
                act.wait_ge(s_df, G_ST[k] + 1)
                nc.scalar.activation(ssq[:, :], rstd[:, :], ACT.Sqrt).then_inc(s_rt, 1)

            def ffn(l):
                gb = G_FF[l]

                def up(g, par):
                    for b in range(2):
                        act.wait_ge(s_df, g + (2 * b + 1))
                        nc.scalar.activation(at[:, b, :], at[:, b, :], ACT.Silu).then_inc(s_silu, 1)
                        act.wait_ge(s_df, g + (2 * b + 2))
                        nc.scalar.activation(gh[:, par, b, :], at[:, b, :], ACT.Copy).then_inc(s_gh, 1)

                up(gb, 0)
                with act.Fori(0, FIT // 2) as i:
                    for s in range(2):
                        up(24 * i + (gb + 4 + 12 * s), 1 - s)
                for m in range(KC):
                    squares(2 * l + 2, m, sq_ffn, s_df, gb + 125 + m)
                    if l == 0:
                        act.dma_start(h_spill[:, m, :], h[:, m, :]).then_inc(s_hsp, 16)
                root(2 * l + 2)

            def proj_out(l):
                act.wait_ge(s_osp, 16 * (KC + NG * l))
                for m in range(OR):
                    act.dma_start(oraw[:, m, :], o_spill[:, m, :]).then_inc(s_old[m], 16)
                for m in range(KC):
                    act.dma_start(h[:, m, :], h_spill[:, m, :]).then_inc(s_hld, 16)
                for m in range(KC):
                    turns = 2 if m % OR < KC - OR else 1
                    act.wait_ge(s_old[m % OR], 16 * (turns * l + m // OR + 1))
                    nc.scalar.activation(oh[:, m, :], oraw[:, m % OR, :], ACT.Copy).then_inc(s_oh, 1)
                    if 0 <= m - 1 < KC - OR:
                        act.wait_ge(s_or, KC * l + m)
                        act.dma_start(oraw[:, m - 1, :], o_spill[:, m - 1 + OR, :]).then_inc(s_old[m - 1], 16)
                for m in range(KC):
                    squares(2 * l + 1, m, sq_wo, s_df, G_WO[l] + m + 1)
                root(2 * l + 1)

            act.dma_start(gains[:, 0, :], A["norm_mix"][0].rearrange("(k p) -> p k", p=P),
                          allow_slow_non_contiguous=True).then_inc(s_const, 16)
            act.dma_start(gains[:, 1, :], A["norm_ffn"][0].rearrange("(k p) -> p k", p=P),
                          allow_slow_non_contiguous=True).then_inc(s_const, 16)
            act.dma_start(gains[:, 2, :], A["norm_mix"][1].rearrange("(k p) -> p k", p=P),
                          allow_slow_non_contiguous=True).then_inc(s_const, 16)
            act.dma_start(gains[:, 3, :], A["norm_ffn"][1].rearrange("(k p) -> p k", p=P),
                          allow_slow_non_contiguous=True).then_inc(s_const, 16)
            act.dma_start(gains[:, 4, :], A["norm_final"].rearrange("(k p) -> p k", p=P),
                          allow_slow_non_contiguous=True).then_inc(s_const, 16)
            for i in range(9):
                n = P if i < 8 else META
                act.wait_ge(s_xt, 2 * i + 2)
                nc.scalar.activation(h[:, 4:8, P * i:P * i + n],
                                     PS[:, 7, 0:4 * n].rearrange("p (c n) -> p c n", n=n),
                                     ACT.Copy).then_inc(s_xrb, 1)
            act.wait_ge(s_const, 80)
            act.wait_ge(s_pad, 2)
            act.wait_ge(s_xrb, 9)
            for m in range(KC):
                squares(0, m, sq_in, s_xra, 9)
            root(0)
            act.wait_ge(s_ur, KC)
            act.wait_ge(s_hsp, 16 * KC)

            act.dma_start(maskb[:, :, :, :], C["mask"]).then_inc(s_na, 16)
            act.dma_start(mb_raw[:, :], A["a_meta_bias"].rearrange("a h m -> a (h m)")
                          .partition_broadcast(P)).then_inc(s_na, 16)
            act.wait_ge(s_zero, 6)
            act.dma_start(bias_rows.rearrange("h c a e -> (h c a e)").rearrange("(p n) -> p n", p=P),
                          vt[:, :, :].rearrange("p a b -> p (a b)")[:, 0:NH * CB * ARR * EW // P]
                          ).then_inc(s_bfill, 16)
            act.wait_ge(s_bfill, 16)
            for c in range(CB):
                act.dma_start(bias_rows[:, c, 4:19, c + 1:c + 32], A["a_rel_bias"][0],
                              allow_slow_non_contiguous=True).then_inc(s_brow, 16)
            act.wait_ge(s_brow, 16 * CB)
            def key_order(p):
                act.wait_ge(s_df, 3 * p + (G_NA + 2))
                act.wait_ge(s_klo, 2 * p)
                act.wait_ge(s_khi, 4 * p)
                grid = keys[:, COLS:COLS + GRID].rearrange("p (r j c) -> p r j c", j=NJ, c=CB)
                nc.scalar.activation(grid, ssq[:, 0:GRID].rearrange("p (j r c) -> p r j c", j=NJ, c=CB),
                                     ACT.Copy).then_inc(s_kn, 1)
                for row in (0, ROWS + 1):
                    for c0 in (8, 32):
                        nc.scalar.activation(keys[:, COLS * row + c0:COLS * row + c0 + META],
                                             ssq[:, GRID:T], ACT.Copy).then_inc(s_kn, 1)

            def k_hi(p):
                act.wait_ge(s_kn, 5 * p + 5)
                act.wait_ge(s_s, TILES * p)
                for hd in range(2):
                    for half in (hd, 1 - hd):
                        nc.scalar.activation(khh[64 * half:64 * half + 64, hd, :],
                                             keys[64 * hd:64 * hd + 64, :], ACT.Copy).then_inc(s_khi, 1)

            def k_lo_copy(p):
                for hd in range(2):
                    act.wait_ge(s_klo, 2 * p + (hd + 1))
                    nc.scalar.activation(kll[64 * (1 - hd):64 * (1 - hd) + 64, hd, :],
                                         kll[64 * hd:64 * hd + 64, hd, :], ACT.Copy).then_inc(s_klc, 1)

            def attend_pair(p, more):
                g = 3 * p + G_NA
                act.wait_ge(s_df, g + 3)
                for hd in range(2):
                    r = slice(64 * hd, 64 * hd + 64)
                    nc.scalar.activation(qs[r, hd, 0:TP], ssq[r, :], ACT.Copy).then_inc(s_qhi, 1)

                def exp(u):
                    w = SN if u % 9 < 8 else WC
                    act.wait_ge(s_sb, TILES * p + (u + 1))
                    nc.scalar.activation(pb[:, u % 3, 0:w], pb[:, u % 3, 0:w], ACT.Exp,
                                         bias=small[:, u % 3, 0:1], scale=-1.0,
                                         accum_out=small[:, u % 3, 1:2]).then_inc(s_ex, 1)

                def t_hi(u):
                    hd, v = u // 9, u % 9
                    act.wait_ge(s_tf, FILLS * p + (u + 7))
                    bank = 3 + u % 2
                    if v == 8:
                        act.wait_ge(s_pv, 10 * p + 5 * hd)
                        nc.scalar.activation(pmh[:, :], PS[:, bank, 0:P], ACT.Copy).then_inc(s_th, 1)
                        return
                    st_ = 4 * hd + v // 2
                    act.wait_ge(s_pv, 10 * p + (5 * ((st_ - 2) // 4) + (st_ - 2) % 4 + 1 if st_ >= 2 else 0))
                    x = v % 2
                    nc.scalar.activation(pth[:, st_ % 2, :, P * x:P * x + P],
                                         PS[:, bank, :].rearrange("p (c n) -> p c n", n=P),
                                         ACT.Copy).then_inc(s_th, 1)

                def o_part(i):
                    act.wait_ge(s_pv, 10 * p + (5 * (i // 3) + (2, 4, 5)[i % 3]))
                    act.wait_ge(s_ob, 6 * p + i)
                    n = 512 if i % 3 < 2 else META
                    nc.scalar.activation(otmp[:, 0:n], PS[64:128, 5, 0:n], ACT.Copy).then_inc(s_oa, 1)

                def v_hi(f):
                    act.wait_ge(s_tf, FILLS * p + (f + 1))
                    act.wait_ge(s_pv, 10 * p)
                    nc.scalar.activation(
                        vst[:, 3 * f:3 * f + 3, :, 0:HD],
                        PS[:, 3 + f % 2, 0:3 * P].rearrange("p (t h d) -> p t h d", t=3, h=2),
                        ACT.Copy).then_inc(s_th, 1)

                v_hi(0)
                v_hi(1)
                exp(0)
                exp(1)
                for f in range(2, 6):
                    v_hi(f)
                o_due = {5: 0, 9: 1, 10: 2, 14: 3}
                for u in range(TILES):
                    t_hi(u)
                    if u + 2 < TILES:
                        exp(u + 2)
                    if u in o_due:
                        o_part(o_due[u])
                o_part(4)
                if more:
                    key_order(p + 1)
                    k_hi(p + 1)
                o_part(5)
                if more:
                    k_lo_copy(p + 1)
                act.wait_ge(s_ob, 6 * p + 6)
                act.dma_start(o_spill[:, bass.ds(p, 1), :].rearrange("p a t -> p (a t)"), ob[:, :]).then_inc(s_osp, 16)

            key_order(0)
            k_hi(0)
            k_lo_copy(0)
            with act.Fori(0, NPAIR - 1) as p:
                attend_pair(p, True)
            attend_pair(NPAIR - 1, False)
            proj_out(0)
            ffn(0)
            act.wait_ge(s_ur, 3 * KC)
            act.wait_ge(s_hsp, 2 * 16 * KC)

            for dst, name in ((cosb[:, :], "cos"), (sinb[:, :], "sin"), (selb[:, :, :], "sel"),
                              (bcb[:, :, :], "bc"), (rotb[:, :], "rot")):
                act.dma_start(dst, C[name]).then_inc(s_gc, 16)
            for e in range(2):
                act.dma_start(gnb[64 * e:64 * e + 64, 0:1], A["b_q_norm"].rearrange("a (d b) -> (a d) b", b=1)).then_inc(s_gc, 16)
            act.dma_start(gnb[0:64, 1:2], A["b_k_norm"].rearrange("a (d b) -> (a d) b", b=1)).then_inc(s_gc2, 16)
            def spill_chunk(g, c, n):
                act.wait_ge(s_rot, n)
                act.dma_start(qkv_spill[g, :, c, :], tq[:, g % 2, c, :]).then_inc(s_qsp[c], 16)
                if g == 0:
                    act.dma_start(qkv_spill[NG, :, c, :], tq[:, 0, c, :]).then_inc(s_qsp[c], 16)

            rots = [(g, c) for what, g, c in order if what == "rot"]
            for n, (what, g, c) in enumerate(order):
                if what == "w":
                    act.wait_ge(s_df, G_GQ + n + 1)
                    nc.scalar.activation(tn[:, g % 2, c, :], tq[:, g % 2, c, :], ACT.Square).then_inc(s_gsq, 1)
                elif what == "sum":
                    act.wait_ge(s_df, G_GQ + n + 1)
                    nc.scalar.activation(nwt[:, 0, :], ssq[:, :], ACT.Sqrt).then_inc(s_gsr, 1)
                elif what == "rot":
                    spill_chunk(g, c, rots.index((g, c)) + 1)
            for spilled in s_qsp:
                act.wait_ge(spilled, 16 * NG + 16)
            act.wait_ge(s_gmem, 2)
            def load(g):
                for c in range(2):
                    act.dma_start(tqb[:, c, :], qkv_spill[bass.ds(g, 1), :, c, :]
                                  .rearrange("a p t -> (a p) t")).then_inc(s_qld, 16)
                act.dma_start(tkv[:, 0:TP], qkv_spill[bass.ds(g, 1), :, 2, :]
                              .rearrange("a p t -> (a p) t")).then_inc(s_qld, 16)

            def set_max(g, par, b):
                n = QB if b < 8 else P
                act.wait_ge(s_mrow, NQB * g + (b + 1))
                nc.scalar.activation(qx[par][64:65, QB * b:QB * b + n], PS[64:65, 4, 0:n],
                                     ACT.Copy).then_inc(s_mset, 1)

            def hi_part(g, par, n):
                if n == 0:
                    act.wait_ge(s_qld, 48 * g + 48)
                    nc.scalar.activation(ks[par][0:64, 0:TP], tkv[0:64, 0:TP], ACT.Copy).then_inc(s_gqh, 1)
                elif n == 1:
                    nc.scalar.activation(kx[par][0:64, 0:T], tkv[0:64, 0:T], ACT.Copy).then_inc(s_gs1, 1)
                else:
                    hh, half = divmod(n - 2, 2)
                    c, e = divmod(hh, 2)
                    src = tqb[64 * e:64 * e + 64, c, :]
                    q = slice(64 * half, 64 * half + 64)
                    m0 = GH * GRID + META * hh
                    nc.scalar.activation(qh[par][q, m0:m0 + META], src[:, GRID:T], ACT.Copy).then_inc(s_gs1, 1)
                    nc.scalar.activation(qh[par][q, GRID * hh:GRID * hh + GRID], src[:, 0:GRID],
                                         ACT.Copy).then_inc(s_gs1 if half == 0 else s_gqh, 1)

            def v_hi(g, par, f):
                act.wait_ge(s_vt, 3 * g + f + 1)
                n = min(4, KT - 4 * f)
                nc.scalar.activation(vg[par][:, 4 * f:4 * f + n, 0:HD],
                                     PS[:, 4, 0:P * n].rearrange("p (t d) -> p t d", t=n)[:, :, HD:P],
                                     ACT.Copy).then_inc(s_vgh, 1)

            def attend(g, par):
                act.wait_ge(s_gql, 5 * g + 5)
                act.wait_ge(s_gqh, 5 * g + 5)
                act.wait_ge(s_vt, 3 * g + 3)
                load(g + 1)

                def p_hi(s):
                    n = QB if s < 8 * KT else P
                    act.wait_ge(s_gex, STEPS * g + (s + 1))
                    if s >= PB:
                        act.wait_ge(s_gpv, STEPS * g + (s - PB + 1))
                    nc.scalar.activation(ph[:, s % PB, 0:n], pf[:, s % PB, 0:n], ACT.Copy).then_inc(s_gph, 1)

                for s in range(STEPS):
                    b, kt = divmod(s, KT)
                    n = QB if b < 8 else P
                    act.wait_ge(s_sc, STEPS * g + (s + 1))
                    if s >= PB:
                        b3, k3_ = divmod(s - PB, KT)
                        act.wait_ge(s_gpl, STEPS * g + (s - PB + 1))
                        act.wait_ge(s_gacc, 8 * NQB * g + (8 * b3 + max(k3_, 1)))
                    q = slice(0, META) if kt == KT - 1 else slice(0, P)
                    nc.scalar.activation(pf[q, s % PB, 0:n], PS[q, 6 + s % 2, 0:n], ACT.Exp).then_inc(s_gex, 1)
                    if kt == ROW_AT:
                        set_max(*((g, par, b + 1) if b < 8 else (g + 1, 1 - par, 0)))
                    if s:
                        p_hi(s - 1)
                    if b and kt == LAG + 1:
                        act.wait_ge(s_gpv, STEPS * g + KT * b)
                        act.wait_ge(s_gob, NQB * g + (b - 1))
                        nc.scalar.activation(ot1[:, :], PS[64:128, OB[(b - 1) % 2], :], ACT.Copy).then_inc(s_goa, 1)
                    if s in H_AT:
                        if s == H_AT[0]:
                            act.wait_ge(s_gpv, STEPS * g)
                        hi_part(g + 1, 1 - par, H_AT.index(s))
                    if kt == 1 and b in V_AT:
                        v_hi(g + 1, 1 - par, V_AT.index(b))
                p_hi(STEPS - 1)
                act.wait_ge(s_gpv, STEPS * g + STEPS)
                act.wait_ge(s_gob, NQB * g + 8)
                nc.scalar.activation(ot1[:, 0:P], PS[64:128, OB[0], 0:P], ACT.Copy).then_inc(s_goa, 1)
            load(0)
            act.wait_ge(s_gz, CLEARS)
            for n in range(10):
                hi_part(0, 0, n)
            for f in range(3):
                v_hi(0, 0, f)
            set_max(0, 0, 0)
            with act.Fori(0, NG // 2) as i:
                for par in range(2):
                    attend(2 * i + par, par)
            proj_out(1)
            ffn(1)
            for i in range(8):
                act.wait_ge(s_ft, 2 * i + 1)
                if i >= 2:
                    act.wait_ge(s_out[i % 2], 16 * (i // 2))
                nc.scalar.activation(fin[:, i % 2, 0:512], PS[:, 6, :], ACT.Copy).then_inc(s_fca, 1)

        @block.vector
        def _(dve):
            def add_square(k, m, buf):
                dve.wait_ge(s_sq, KC * k + m + 1)
                if m == 0:
                    ins = nc.vector.tensor_copy(ssq[:, :], buf[:, 0, :])
                else:
                    dve.wait_ge(s_acc, (KC - 1) * k + m)
                    ins = nc.vector.tensor_tensor(ssq[:, :], ssq[:, :], buf[:, m % 2, :], ALU.add)
                ins.then_inc(s_ssq if m == KC - 1 else s_acc, 1)
                if k < 4:
                    dve.wait_ge(s_uh, KC * k + m + 1)
                    nc.vector.scalar_tensor_tensor(ul[:, m, :], h[:, m, :], gains[:, k, m:m + 1],
                                                   uh[:, m, :].bitcast(F32), op0=ALU.mult,
                                                   op1=ALU.subtract).then_inc(s_ur, 1)

            def refine(v, y, t, n):
                nc.vector.reciprocal(y, y).then_inc(s_nw, 1)
                dve.wait_ge(s_nw, 4 * n + 1)
                nc.vector.scalar_tensor_tensor(t, y, -0.5, y, op0=ALU.mult, op1=ALU.mult).then_inc(s_nw, 1)
                dve.wait_ge(s_nw, 4 * n + 2)
                nc.vector.tensor_tensor(t, t, v, ALU.mult).then_inc(s_nw, 1)
                dve.wait_ge(s_nw, 4 * n + 3)
                nc.vector.tensor_scalar(t, t, 1.5, None, ALU.add).then_inc(s_nw, 1)
                dve.wait_ge(s_nw, 4 * n + 4)
                return nc.vector.tensor_tensor(v, y, t, ALU.mult)

            def rsqrt(k, buf):
                dve.wait_ge(s_st, k + 1)
                nc.vector.tensor_scalar(banks(rstd[:, :]), PS[:, D1:D1 + NB, 0:CW], 1.0 / D, EPS,
                                        ALU.mult, ALU.add).then_inc(s_df, 1)
                dve.wait_ge(s_rt, k + 1)
                n = k + (NG if k > 2 else 0)
                refine(rstd[:, :], ssq[:, :], buf[:, 0, :], n).then_inc(s_rs, 1)
                dve.wait_ge(s_rs, k + 1)

            def add_to_h(m, set_, need_sem, need):
                dve.wait_ge(need_sem, need)
                hm = banks(h[:, m, :])
                nc.vector.tensor_tensor(hm, PS[:, set_:set_ + NB, 0:CW], hm, ALU.add).then_inc(s_df, 1)

            def ffn(l):
                ub, gb = U_FF[l], G_FF[l]

                def up(n, g, k, par):
                    for b in range(2):
                        a3 = banks(at[:, b, :])
                        dve.wait_ge(s_un, n + (4 * b + 2))
                        dve.wait_ge(s_gr, k + b)
                        nc.vector.tensor_tensor(a3, PS[:, D0:D0 + NB, 0:CW], banks(rstd[:, :]),
                                                ALU.mult).then_inc(s_df, 1)
                        dve.wait_ge(s_silu, k + (b + 1))
                        nc.vector.tensor_tensor(at[:, b, :], at[:, b, :], rstd[:, :], ALU.mult).then_inc(s_sr, 1)
                        dve.wait_ge(s_sr, k + (b + 1))
                        dve.wait_ge(s_un, n + (4 * b + 4))
                        nc.vector.tensor_tensor(a3, PS[:, D1:D1 + NB, 0:CW], a3, ALU.mult).then_inc(s_df, 1)
                        dve.wait_ge(s_gh, k + (b + 1))
                        nc.vector.tensor_tensor(gl[:, par, b, :], at[:, b, :], gh[:, par, b, :].bitcast(F32),
                                                ALU.subtract).then_inc(s_gr, 1)

                def down(n, g):
                    for m in range(KC):
                        if m == 0:
                            dve.wait_ge(s_df, g)
                        add_to_h(m, D1 if m % 2 else D0, s_un, n + (m + 1))

                k0 = 2 * FIT * l
                up(ub, gb, k0, 0)
                with dve.Fori(0, FIT // 2) as i:
                    for s in range(2):
                        up(32 * i + (ub + 8 + 16 * s), None, 4 * i + (k0 + 2 + 2 * s), 1 - s)
                        down(32 * i + (ub + 16 + 16 * s), 24 * i + (gb + 8 + 12 * s))
                k = 2 * l + 2
                dve.wait_ge(s_df, gb + 124)
                for m in range(KC):
                    add_to_h(m, D1 if m % 2 else D0, s_un, ub + 168 + m + 1)
                    if m:
                        add_square(k, m - 1, sq_ffn)
                add_square(k, KC - 1, sq_ffn)
                rsqrt(k, sq_ffn)

            def proj_out(l):
                for m in range(KC):
                    dve.wait_ge(s_oh, KC * l + m + 1)
                    nc.vector.tensor_tensor(ol[:, m, :], oraw[:, m % OR, :], oh[:, m, :].bitcast(F32),
                                            ALU.subtract).then_inc(s_or, 1)
                dve.wait_ge(s_hld, 16 * KC * (l + 1))
                for m in range(KC):
                    add_to_h(m, D1 if m % 2 else D0, s_un, U_WO[l] + 2 * m + 2)
                    if m:
                        add_square(2 * l + 1, m - 1, sq_wo)
                add_square(2 * l + 1, KC - 1, sq_wo)
                rsqrt(2 * l + 1, sq_wo)

            nc.vector.memset(ones[:, :], 1.0).then_inc(s_pad, 1)
            nc.vector.memset(h[:, :, T:TP], 0.0).then_inc(s_pad, 1)
            for i in range(9):
                n = P if i < 8 else META
                dve.wait_ge(s_xt, 2 * i + 1)
                nc.vector.tensor_copy(h[:, 0:4, P * i:P * i + n],
                                      PS[:, 6, 0:4 * n].rearrange("p (c n) -> p c n", n=n)).then_inc(s_xra, 1)
            dve.wait_ge(s_const, 80)
            dve.wait_ge(s_pad, 2)
            dve.wait_ge(s_xra, 9)
            for m in range(KC):
                add_square(0, m, sq_in)
            rsqrt(0, sq_in)

            def take_v(p):
                dve.wait_ge(s_un, 6 * p + 2)
                dve.wait_ge(s_vs, 12 * p)
                nc.vector.tensor_tensor(banks(vals[:, :]), PS[:, D0:D0 + NB, 0:CW], banks(rstd[:, :]),
                                        ALU.mult).then_inc(s_df, 1)

            def take_k(p):
                dve.wait_ge(s_un, 6 * p + 4)
                dve.wait_ge(s_qhi, 2 * p)
                dve.wait_ge(s_qlo, 2 * p)
                nc.vector.tensor_tensor(banks(ssq[:, :]), PS[:, D0:D0 + NB, 0:CW], banks(rstd[:, :]),
                                        ALU.mult).then_inc(s_df, 1)

            def k_lo(p):
                dve.wait_ge(s_s, TILES * p)
                dve.wait_ge(s_klc, 2 * p)
                for hd in range(2):
                    r = slice(64 * hd, 64 * hd + 64)
                    dve.wait_ge(s_khi, 4 * p + (2 * hd + 1))
                    nc.vector.tensor_tensor(kll[r, hd, :], keys[r, :], khh[r, hd, :].bitcast(F32),
                                            ALU.subtract).then_inc(s_klo, 1)

            def attend_pair(p, more):
                dve.wait_ge(s_un, 6 * p + 6)
                dve.wait_ge(s_kn, 5 * p + 5)
                nc.vector.scalar_tensor_tensor(banks(ssq[:, :]), PS[:, D0:D0 + NB, 0:CW], -HD ** -0.5,
                                               banks(rstd[:, :]), op0=ALU.mult, op1=ALU.mult).then_inc(s_df, 1)
                for hd in range(2):
                    r = slice(64 * hd, 64 * hd + 64)
                    r2 = slice(64 - 64 * hd, 128 - 64 * hd)
                    dve.wait_ge(s_qhi, 2 * p + (hd + 1))
                    nc.vector.tensor_tensor(qs[r2, hd, 0:TP], ssq[r, :], qs[r, hd, 0:TP].bitcast(F32),
                                            ALU.subtract).then_inc(s_qlo, 1)

                def bias(u):
                    w = SN if u % 9 < 8 else WC
                    dve.wait_ge(s_s, TILES * p + (u + 1))
                    dve.wait_ge(s_bm, 34 * p + (2 * (u + 1) - (u >= 8) - (u >= 17)))
                    dve.wait_ge(s_tf, FILLS * p + max(u + 4, 0) if u >= 3 else FILLS * p)
                    nc.vector.memset(small[:, u % 3, 3:4], 0.0).then_inc(s_car, 1)
                    nc.vector.tensor_tensor_reduce(pb[:, u % 3, 0:w], PS[:, 6 + u % 2, 0:w], bm[:, u % 3, 0:w],
                                                   1.0, 3e38, ALU.add, ALU.min,
                                                   small[:, u % 3, 0:1]).then_inc(s_sb, 1)

                def norm(u):
                    w = SN if u % 9 < 8 else WC
                    dve.wait_ge(s_ex, TILES * p + (u + 1))
                    nc.vector.reciprocal(small[:, u % 3, 2:3], small[:, u % 3, 1:2]).then_inc(s_dv, 1)
                    dve.wait_ge(s_dv, TILES * p + (u + 1))
                    nc.vector.tensor_scalar(pb[:, u % 3, 0:w], pb[:, u % 3, 0:w], small[:, u % 3, 2:3], None,
                                            ALU.mult).then_inc(s_pr, 1)

                def t_lo(u):
                    hd, v = u // 9, u % 9
                    bank = 3 + u % 2
                    dve.wait_ge(s_th, FILLS * p + (u + 7))
                    if v == 8:
                        nc.vector.tensor_tensor(pml[:, :], PS[:, bank, 0:P], pmh[:, :].bitcast(F32),
                                                ALU.subtract).then_inc(s_tl, 1)
                        return
                    st_, x = 4 * hd + v // 2, v % 2
                    nc.vector.tensor_tensor(ptl[:, st_ % 2, :, P * x:P * x + P],
                                            PS[:, bank, :].rearrange("p (c n) -> p c n", n=P),
                                            pth[:, st_ % 2, :, P * x:P * x + P].bitcast(F32),
                                            ALU.subtract).then_inc(s_tl, 1)

                def o_sum(i):
                    hd, w = i // 3, i % 3
                    n = 512 if w < 2 else META
                    dve.wait_ge(s_oa, 6 * p + (i + 1))
                    dve.wait_ge(s_osp, 16 * p)
                    nc.vector.tensor_tensor(ob[64 * hd:64 * hd + 64, 512 * w:512 * w + n], PS[0:64, 5, 0:n],
                                            otmp[:, 0:n], ALU.add).then_inc(s_ob, 1)

                def v_lo(f):
                    dve.wait_ge(s_th, FILLS * p + (f + 1))
                    nc.vector.tensor_tensor(
                        vst[:, 3 * f:3 * f + 3, :, HD:P],
                        PS[:, 3 + f % 2, 0:3 * P].rearrange("p (t h d) -> p t h d", t=3, h=2),
                        vst[:, 3 * f:3 * f + 3, :, 0:HD].bitcast(F32), ALU.subtract).then_inc(s_tl, 1)

                v_lo(0)
                v_lo(1)
                bias(0)
                norm(0)
                bias(1)
                norm(1)
                for f in range(2, 6):
                    v_lo(f)
                o_due = {5: 0, 9: 1, 10: 2, 14: 3}
                for u in range(TILES):
                    if more and u == 8:
                        take_v(p + 1)
                    if more and u == 17:
                        take_k(p + 1)
                    if u + 2 < TILES:
                        bias(u + 2)
                    t_lo(u)
                    if u + 2 < TILES:
                        norm(u + 2)
                    if u in o_due:
                        o_sum(o_due[u])
                o_sum(4)
                if more:
                    k_lo(p + 1)
                o_sum(5)

            dve.wait_ge(s_hsp, 16 * KC)
            take_v(0)
            dve.wait_ge(s_zero, 6)
            dve.wait_ge(s_na, 32)
            for cls, at_ in ((0, 8), (1, 0)):
                nc.vector.tensor_scalar(mbn[:, :, cls, at_:at_ + META],
                                        mb_raw[:, :].rearrange("p (h m) -> p h m", m=META), -1.0, None,
                                        ALU.mult).then_inc(s_mbn, 1)
            take_k(0)
            k_lo(0)
            with dve.Fori(0, NPAIR - 1) as p:
                attend_pair(p, True)
            attend_pair(NPAIR - 1, False)
            proj_out(0)
            ffn(0)

            dve.wait_ge(s_hsp, 16 * KC * 2)
            dve.wait_ge(s_gc, 16 * 7)
            dve.wait_ge(s_gc2, 16)
            nc.vector.tensor_scalar(gnb[:, 0:1], gnb[:, 0:1], HD ** -0.5, None, ALU.mult).then_inc(s_gnb, 1)
            dve.wait_ge(s_gnb, 1)
            for n, (what, g, c) in enumerate(order):
                set_ = D1 if n % 2 else D0
                aux = sum(w != "w" for w, _, _ in order[:n])
                q = slice(0, 64) if c == 2 else slice(0, P)
                raw, t = tq[q, g % 2, c, :], tn[q, g % 2, c, :]
                if what == "w":
                    dve.wait_ge(s_un, 6 * g + (U_GQ + 2 * c + 2))
                    if g >= 2:
                        dve.wait_ge(s_qsp[c], 16 * g)
                    nc.vector.tensor_tensor(banks(tq[:, g % 2, c, :]), PS[:, set_:set_ + NB, 0:CW],
                                            banks(rstd[:, :]), ALU.mult).then_inc(s_df, 1)
                    continue
                dve.wait_ge(s_ga, aux + 1)
                if what == "sum":
                    nc.vector.tensor_scalar(banks(ssq[:, :]), PS[:, set_:set_ + NB, 0:CW], 1.0 / HD, EPS,
                                            ALU.mult, ALU.add).then_inc(s_df, 1)
                    dve.wait_ge(s_gsr, g + 1)
                    refine(ssq[:, :], nwt[:, 0, :], nwt[:, 1, :], 3 + g).then_inc(s_grc, 1)
                elif what == "spread":
                    gain = gnb[q, 1:2] if c == 2 else gnb[q, 0:1]
                    nc.vector.scalar_tensor_tensor(banks(t), banks(raw), gain, PS[q, set_:set_ + NB, 0:CW],
                                                   op0=ALU.mult, op1=ALU.mult).then_inc(s_df, 1)
                    dve.wait_ge(s_df, G_GQ + n + 1)
                    nc.vector.tensor_tensor(raw, t, cosb[q, :], ALU.mult).then_inc(s_cs, 1)
                else:
                    dve.wait_ge(s_cs, sum(w == "spread" for w, _, _ in order[:n]))
                    nc.vector.tensor_tensor(banks(t), PS[q, set_:set_ + NB, 0:CW], banks(sinb[q, :]),
                                            ALU.mult).then_inc(s_df, 1)
                    dve.wait_ge(s_df, G_GQ + n + 1)
                    nc.vector.tensor_tensor(raw, raw, t, ALU.add).then_inc(s_rot, 1)
            dve.wait_ge(s_gmem, 2)
            zero = ob2[:, :, :].rearrange("p a t -> p (a t)")
            m0 = GH * GRID + GH * META
            for par in range(2):
                clear = [qh[par][:, m0:QW], qx[par][0:64, m0:QW], ks[par][:, TP:TW], kx[par][0:64, T:TW],
                         kx[par][64:P, :]]
                clear += [qx[par][64:P, a:min(a + 2 * TP, QW)] for a in range(0, QW, 2 * TP)]
                for t in clear:
                    base = 0 if t.shape[0] == P or t.shape[1] < TP and t.shape[0] == 64 else 64
                    nc.vector.tensor_copy(t, zero[base:base + t.shape[0], 0:t.shape[1]]).then_inc(s_gz, 1)
            nc.vector.tensor_copy(ones_r[:, :], ones[:, :]).then_inc(s_gz, 1)
            dve.wait_ge(s_gz, CLEARS - 2)
            for par in range(2):
                nc.vector.tensor_scalar(kx[par][64:65, 0:T], zero[64:65, 0:T], 1.0, None,
                                        ALU.add).then_inc(s_gz, 1)
            def take_max(g, b, i):
                t = 4 * b + i
                dve.wait_ge(s_mx, MT * g + (t + 1))
                dve.wait_ge(s_mrow, NQB * g + b)
                nc.vector.tensor_reduce(nmx[:, i:i + 1], PS[:, 0:3, 0:CW], AX.XY, ALU.max,
                                        negate=True).then_inc(s_mr, 1)
                dve.wait_ge(s_mr, MT * g + (t + 1))
                nc.vector.tensor_scalar(dgm[:, i, :], ident[:, :], nmx[:, i:i + 1], None,
                                        ALU.mult).then_inc(s_dg, 1)

            def lo_part(g, par, n):
                dve.wait_ge(s_gqh, 5 * g + (n + 1))
                if n == 0:
                    nc.vector.tensor_tensor(ks[par][64:128, 0:TP], tkv[0:64, 0:TP],
                                            ks[par][0:64, 0:TP].bitcast(F32), ALU.subtract).then_inc(s_gql, 1)
                    return
                hh = n - 1
                c, e = divmod(hh, 2)
                r = slice(64 * e, 64 * e + 64)
                m0 = GH * GRID + META * hh
                nc.vector.tensor_tensor(qx[par][0:64, m0:m0 + META], tqb[r, c, GRID:T],
                                        qh[par][r, m0:m0 + META].bitcast(F32), ALU.subtract).then_inc(s_gs2, 1)
                nc.vector.tensor_tensor(qx[par][0:64, GRID * hh:GRID * hh + GRID], tqb[r, c, 0:GRID],
                                        qh[par][r, GRID * hh:GRID * hh + GRID].bitcast(F32),
                                        ALU.subtract).then_inc(s_gql, 1)

            def v_lo(g, par, f):
                dve.wait_ge(s_vgh, 3 * g + f + 1)
                n = min(4, KT - 4 * f)
                nc.vector.tensor_tensor(vg[par][:, 4 * f:4 * f + n, HD:P],
                                        PS[:, 4, 0:P * n].rearrange("p (t d) -> p t d", t=n)[:, :, HD:P],
                                        vg[par][:, 4 * f:4 * f + n, 0:HD].bitcast(F32),
                                        ALU.subtract).then_inc(s_vgl, 1)

            def attend(g, par):
                def divide(b):
                    nt = 4 if b < 8 else 1
                    dve.wait_ge(s_gsum, NQB * g + (b + 1))
                    nc.vector.reciprocal(rsm[:, 0:nt], PS[:, 4, 0:nt]).then_inc(s_rsm, 1)
                    dve.wait_ge(s_rsm, NQB * g + (b + 1))
                    for i in range(nt):
                        nc.vector.tensor_scalar(dgs[:, i, :], ident[:, :], rsm[:, i:i + 1], None,
                                                ALU.mult).then_inc(s_gdr if i == nt - 1 else s_gds, 1)

                def o_block(b):
                    n = QB if b < 8 else P
                    dve.wait_ge(s_goa, NQB * g + (b + 1))
                    dve.wait_ge(s_gspr, NQB * g + (b + 1))
                    nc.vector.tensor_tensor(ot1[:, 0:n], PS[0:64, OB[b % 2], 0:n], ot1[:, 0:n], ALU.add).then_inc(s_got, 1)
                    dve.wait_ge(s_got, NQB * g + (b + 1))
                    dve.wait_ge(s_osp, 16 * g + 16 * KC)
                    if b < 8:
                        hh, half = divmod(b, 2)
                        c, e = divmod(hh, 2)
                        nc.vector.tensor_tensor(ob2[64 * e:64 * e + 64, c, QB * half:QB * half + QB],
                                                ot1[:, :], PS[0:64, 4, :], ALU.mult).then_inc(s_gob, 1)
                        return
                    for hh in range(GH):
                        c, e = divmod(hh, 2)
                        m = slice(META * hh, META * hh + META)
                        nc.vector.tensor_tensor(ob2[64 * e:64 * e + 64, c, GRID:T], ot1[:, m],
                                                PS[0:64, 4, m], ALU.mult).then_inc(s_gob if hh == 3 else s_gs2, 1)

                def p_lo(s):
                    n = QB if s < 8 * KT else P
                    dve.wait_ge(s_gph, STEPS * g + (s + 1))
                    nc.vector.tensor_tensor(pl[:, s % PB, 0:n], pf[:, s % PB, 0:n], ph[:, s % PB, 0:n].bitcast(F32),
                                            ALU.subtract).then_inc(s_gpl, 1)

                for s in range(STEPS):
                    b, kt = divmod(s, KT)
                    if kt in M_AT and not (b == 7 and kt):
                        take_max(*((g, b + 1) if b < 8 else (g + 1, 0)), M_AT.index(kt))
                    if s:
                        p_lo(s - 1)
                    if kt == 2 and b in V_AT:
                        v_lo(g + 1, 1 - par, V_AT.index(b))
                    if s in L_AT:
                        if s == L_AT[0]:
                            dve.wait_ge(s_gpv, STEPS * g)
                        lo_part(g + 1, 1 - par, L_AT.index(s))
                    if b and kt == LAG - 1:
                        divide(b - 1)
                    if b and kt == LAG + 1:
                        o_block(b - 1)
                p_lo(STEPS - 1)
                divide(8)
                o_block(8)
            for n in range(5):
                lo_part(0, 0, n)
            for f in range(3):
                v_lo(0, 0, f)
            for i in range(4):
                take_max(0, 0, i)
            with dve.Fori(0, NG // 2) as i:
                for par in range(2):
                    attend(2 * i + par, par)
            proj_out(1)
            ffn(1)
            dve.wait_ge(s_rs, 5)
            for half in (slice(0, GRID // 2), slice(GRID // 2, GRID)):
                for m in range(KC):
                    nc.vector.scalar_tensor_tensor(h[:, m, half], h[:, m, half], gains[:, 4, m:m + 1],
                                                   rstd[:, half], op0=ALU.mult,
                                                   op1=ALU.mult).then_inc(s_fs, 1)
            for i in range(8):
                dve.wait_ge(s_ft, 2 * i + 2)
                if i >= 2:
                    dve.wait_ge(s_out[i % 2], 16 * (i // 2))
                nc.vector.tensor_copy(fin[:, i % 2, 512:1024], PS[:, 7, :]).then_inc(s_fcb, 1)


def tables():
    q = np.arange(P)
    mask = np.zeros((P, 2, NJ, WR, WC), np.float32)
    for x in range(2):
        r = HR * x + q // CB
        kr = np.arange(WR) + 4 * x
        rs = np.clip(r - WIN_R // 2, 0, ROWS - WIN_R)
        row_ok = (kr >= rs[:, None]) & (kr < rs[:, None] + WIN_R)
        for j in range(NJ):
            c = CB * j + q % CB
            kc = np.arange(WC) + K0[j]
            cs = np.clip(c - WIN_C // 2, 0, COLS - WIN_C)
            col_ok = (kc >= cs[:, None]) & (kc < cs[:, None] + WIN_C)
            mask[:, x, j] = np.where(row_ok[:, :, None] & col_ok[:, None, :], 0.0, NEG)
    t = np.arange(GRID)
    row = np.zeros(TP, np.float32)
    col = np.zeros(TP, np.float32)
    row[:GRID] = (t // CB) % ROWS
    col[:GRID] = CB * (t // (CB * ROWS)) + t % CB
    sec = HD // 2
    freqs = (1.0 / (np.float32(10000.0) ** (np.arange(0, sec, 2, dtype=np.float32) / np.float32(sec)))).astype(np.float32)
    d = np.arange(P) % HD
    ang = np.where((d < sec)[:, None], row[None], col[None]) * freqs[d % (sec // 2)][:, None]
    rot = np.zeros((P, P), np.float32)
    for m in range(P):
        if m % sec < sec // 2:
            rot[m + sec // 2, m] = -1.0
        else:
            rot[m - sec // 2, m] = 1.0
    sel = np.zeros((P, 3, P), np.float32)
    for c in range(3):
        for e in range(2 if c < 2 else 1):
            sel[64 * e:64 * e + 64, c, 2 * c + e] = 1.0
    return {
        "ident": np.eye(P, dtype=np.float32),
        "mask": mask.reshape(P, 2, NJ, WR * WC).astype(mybir.dt.np(BF16)),
        "cos": np.cos(ang.astype(np.float32)).astype(np.float32),
        "sin": np.sin(ang.astype(np.float32)).astype(np.float32),
        "rot": rot,
        "sel": sel,
        "bc": np.ascontiguousarray(sel.transpose(2, 1, 0)),
    }


_INS = ["x", "meta_tokens", "norm_mix", "norm_ffn", "norm_final", "a_w_qkv", "a_rel_bias", "a_meta_bias",
        "a_w_o", "b_w_qkv", "b_q_norm", "b_k_norm", "b_w_o", "ffn_w1", "ffn_w3", "ffn_w2"]


def kernel(**inputs):
    import concourse.bacc as bacc
    from concourse.bass_utils import run_bass_kernel_spmd as run

    nc = bacc.Bacc("TRN2", target_bir_lowering=False, num_devices=1)
    arrays, given, consts = {}, {}, {}
    for name in _INS:
        a = np.ascontiguousarray(inputs[name])
        arrays[f"in_{name}"] = a
        given[name] = nc.dram_tensor(f"in_{name}", a.shape, mybir.dt.from_np(a.dtype), kind="ExternalInput").ap()
    for name, a in tables().items():
        arrays[f"table_{name}"] = a
        consts[name] = nc.dram_tensor(f"table_{name}", a.shape, mybir.dt.from_np(a.dtype), kind="ExternalInput").ap()
    out = nc.dram_tensor("out_0", (1, GRID, D), F32, kind="ExternalOutput").ap()
    build(nc, given, consts, out)
    return run(nc, [arrays], core_ids=[0]).results[0]["out_0"]
```
